# Optimizing a Trainium2 kernel written in Bass

```python
import jax, jax.numpy as jnp
from jax import lax
import numpy as np

D_MODEL = 1024
BATCH = 1
SEQ = 256
DEPTH = 2
DEC_BATCH = 8
DEC_SEQ = 4
PAST_LEN = 2048
PAGE_SIZE = 128

D_A = D_MODEL // 2
D_B = D_MODEL // 2
CONV_A_WIDTH = 31
CONV_B_WIDTH = 3
POOL_WINDOWS = (2, 4, 8, 16)
N_POOL_GROUPS = len(POOL_WINDOWS)
POOL_GROUP = D_MODEL // N_POOL_GROUPS
POOL_HIST = max(POOL_WINDOWS) - 1
D_FF = 256 * ((8 * D_MODEL // 3 + 255) // 256)
N_EVEN = (DEPTH + 1) // 2
N_ODD = DEPTH // 2
EPS = 1e-6

kernel_name = "hybrid_conv_pool_macaron_decode_step"

def rmsnorm(x, g):
    xf = x.astype(jnp.float32)
    y = xf * lax.rsqrt(jnp.mean(xf * xf, axis=-1, keepdims=True) + EPS)
    return (y * g.astype(jnp.float32)).astype(x.dtype)

def layernorm(x, g, b):
    xf = x.astype(jnp.float32)
    mu = jnp.mean(xf, axis=-1, keepdims=True)
    xc = xf - mu
    y = xc * lax.rsqrt(jnp.mean(xc * xc, axis=-1, keepdims=True) + EPS)
    return (y * g.astype(jnp.float32) + b.astype(jnp.float32)).astype(x.dtype)

def swiglu(h, w_in, w_out):
    gate, up = jnp.split(h @ w_in, 2, axis=-1)
    return (jax.nn.silu(gate) * up) @ w_out

def causal_dwconv(ext, w):
    return lax.conv_general_dilated(
        ext, w[:, None, :].astype(ext.dtype), window_strides=(1,), padding='VALID',
        dimension_numbers=('NWC', 'WIO', 'NWC'), feature_group_count=ext.shape[-1])

def conv_heads_mixer(h, hist_a, hist_b, w_in, conv_a_w, conv_a_b, ln_a_g, ln_a_b, conv_b_w, w_out):
    z = h @ w_in
    a_val, a_gate, b_gate, c_gate, v = jnp.split(z, [D_A, 2 * D_A, 2 * D_A + D_B, 2 * D_A + 2 * D_B], axis=-1)
    ua = a_val * jax.nn.sigmoid(a_gate)
    ext_a = jnp.concatenate([hist_a.astype(ua.dtype), ua], axis=1)
    ya = causal_dwconv(ext_a, conv_a_w) + conv_a_b.astype(ua.dtype)
    ya = jax.nn.silu(layernorm(ya, ln_a_g, ln_a_b))
    ub = c_gate * v
    ext_b = jnp.concatenate([hist_b.astype(ub.dtype), ub], axis=1)
    yb = b_gate * causal_dwconv(ext_b, conv_b_w)
    out = jnp.concatenate([ya, yb], axis=-1) @ w_out
    return out, ext_a[:, -(CONV_A_WIDTH - 1):], ext_b[:, -(CONV_B_WIDTH - 1):]

def pool_mixer(h, hist, pos0, pool_w, pool_b, pool_scale):
    T = h.shape[1]
    ext = jnp.concatenate([hist.astype(h.dtype), h], axis=1)
    cs = jnp.pad(jnp.cumsum(ext.astype(jnp.float32), axis=1), ((0, 0), (1, 0), (0, 0)))
    pos = (pos0 + jnp.arange(T)).astype(jnp.float32)
    means = []
    for g, w in enumerate(POOL_WINDOWS):
        sl = slice(g * POOL_GROUP, (g + 1) * POOL_GROUP)
        end = cs[:, POOL_HIST + 1:POOL_HIST + 1 + T, sl]
        start = cs[:, POOL_HIST + 1 - w:POOL_HIST + 1 - w + T, sl]
        count = jnp.minimum(pos + 1.0, float(w))[None, :, None]
        means.append((end - start) / count)
    pooled = jnp.concatenate(means, axis=-1) - h.astype(jnp.float32)
    pg = pooled.reshape(pooled.shape[0], T, N_POOL_GROUPS, POOL_GROUP)
    mixed = jnp.einsum('btgc,gcd->btgd', pg, pool_w.astype(jnp.float32)).reshape(pooled.shape)
    out = (mixed + pool_b.astype(jnp.float32)) * pool_scale.astype(jnp.float32)
    return out.astype(h.dtype), ext[:, -POOL_HIST:]

def setup_inputs(seed: int = 0) -> dict:
    key = jax.random.key(seed)
    ks = jax.random.split(key, 24)
    f32 = jnp.float32
    nrm = lambda k, shape, s: jax.random.normal(k, shape, f32) * s
    return {
        "x_prompt": nrm(ks[0], (BATCH, SEQ, D_MODEL), 1.0),
        "x_sample": nrm(ks[1], (DEC_BATCH, DEC_SEQ, D_MODEL), 1.0),
        "state_conv_a": nrm(ks[2], (N_EVEN, DEC_BATCH, CONV_A_WIDTH - 1, D_A), 0.5),
        "state_conv_b": nrm(ks[3], (N_EVEN, DEC_BATCH, CONV_B_WIDTH - 1, D_B), 0.5),
        "state_pool": nrm(ks[4], (N_ODD, DEC_BATCH, POOL_HIST, D_MODEL), 1.0),
        "norm_g": 1.0 + nrm(ks[5], (DEPTH, 3, D_MODEL), 0.02),
        "ffn_w_in": nrm(ks[6], (DEPTH, 2, D_MODEL, 2 * D_FF), D_MODEL ** -0.5),
        "ffn_w_out": nrm(ks[7], (DEPTH, 2, D_FF, D_MODEL), D_FF ** -0.5),
        "mix_w_in": nrm(ks[8], (N_EVEN, D_MODEL, 2 * D_A + 3 * D_B), D_MODEL ** -0.5),
        "conv_a_w": nrm(ks[9], (N_EVEN, CONV_A_WIDTH, D_A), CONV_A_WIDTH ** -0.5),
        "conv_a_b": nrm(ks[10], (N_EVEN, D_A), 0.02),
        "ln_a_g": 1.0 + nrm(ks[11], (N_EVEN, D_A), 0.02),
        "ln_a_b": nrm(ks[12], (N_EVEN, D_A), 0.02),
        "conv_b_w": nrm(ks[13], (N_EVEN, CONV_B_WIDTH, D_B), CONV_B_WIDTH ** -0.5),
        "mix_w_out": nrm(ks[14], (N_EVEN, D_A + D_B, D_MODEL), (D_A + D_B) ** -0.5),
        "pool_w": nrm(ks[15], (N_ODD, N_POOL_GROUPS, POOL_GROUP, POOL_GROUP), POOL_GROUP ** -0.5),
        "pool_b": nrm(ks[16], (N_ODD, D_MODEL), 0.02),
        "pool_scale": 0.5 + nrm(ks[17], (N_ODD, D_MODEL), 0.05),
        "final_norm_g": 1.0 + nrm(ks[18], (D_MODEL,), 0.02),
    }

def reference(x_prompt, x_sample, state_conv_a, state_conv_b, state_pool,
              norm_g, ffn_w_in, ffn_w_out, mix_w_in, conv_a_w, conv_a_b, ln_a_g, ln_a_b,
              conv_b_w, mix_w_out, pool_w, pool_b, pool_scale, final_norm_g):

    def run_group(x, hist_a, hist_b, hist_pool, pos0):
        new_a, new_b, new_p = [], [], []
        for l in range(DEPTH):
            x = x + 0.5 * swiglu(rmsnorm(x, norm_g[l, 0]), ffn_w_in[l, 0], ffn_w_out[l, 0])
            h = rmsnorm(x, norm_g[l, 1])
            if l % 2 == 0:
                e = l // 2
                m, ha, hb = conv_heads_mixer(h, hist_a[e], hist_b[e], mix_w_in[e], conv_a_w[e], conv_a_b[e],
                                             ln_a_g[e], ln_a_b[e], conv_b_w[e], mix_w_out[e])
                new_a.append(ha)
                new_b.append(hb)
            else:
                o = l // 2
                m, hp = pool_mixer(h, hist_pool[o], pos0, pool_w[o], pool_b[o], pool_scale[o])
                new_p.append(hp)
            x = x + m
            x = x + 0.5 * swiglu(rmsnorm(x, norm_g[l, 2]), ffn_w_in[l, 1], ffn_w_out[l, 1])
        y = rmsnorm(x, final_norm_g)
        return y, jnp.stack(new_a, axis=0), jnp.stack(new_b, axis=0), jnp.stack(new_p, axis=0)

    dt = x_prompt.dtype
    zero_a = jnp.zeros((N_EVEN, BATCH, CONV_A_WIDTH - 1, D_A), dt)
    zero_b = jnp.zeros((N_EVEN, BATCH, CONV_B_WIDTH - 1, D_B), dt)
    zero_p = jnp.zeros((N_ODD, BATCH, POOL_HIST, D_MODEL), dt)
    y_prompt, pa, pb, pp = run_group(x_prompt, zero_a, zero_b, zero_p, 0)
    y_sample, sa, sb, sp = run_group(x_sample, state_conv_a, state_conv_b, state_pool, PAST_LEN)
    return (y_prompt, y_sample, pa, pb, pp, sa, sb, sp)


_drawn_inputs = setup_inputs


def setup_inputs(seed=0):
    import zlib

    import numpy as np

    out = dict(_drawn_inputs(seed))
    spreads = {}
    factors = {'conv_a_b': 3.808, 'ln_a_g': 6.301, 'ln_a_b': 8.0, 'pool_b': 7.922, 'final_norm_g': 2.905}
    for name, (base, spread) in spreads.items():
        noise = np.random.default_rng([zlib.crc32(name.encode()), seed]).standard_normal(out[name].shape)
        drawn = base * np.exp(spread * noise) if base else spread * noise
        out[name] = __import__('jax').numpy.asarray(drawn.astype(out[name].dtype))
    for name, factor in factors.items():
        out[name] = (out[name] * factor).astype(out[name].dtype)
    return out
```

```python
from contextlib import ExitStack

import concourse.bass as bass
from concourse import mybir

F32 = mybir.dt.float32
F32R = mybir.dt.float32r
ALU = mybir.AluOpType
ACT = mybir.ActivationFunctionType

P = 128
PROMPT, SEQS, STEP = 256, 8, 4
T = PROMPT + SEQS * STEP
D = 1024
KD = D // P
DFF = 2816
KF = DFF // P
DA = 512
KA = DA // P
TAPS_A, TAPS_B = 31, 3
HA, HB, HC = TAPS_A - 1, TAPS_B - 1, 15
WINDOWS = (2, 4, 8, 16)
EPS = 1e-6

RING, SLOT = 4, 2048
UNITS = KF // 2
IN_CHUNKS = 2 * UNITS
QUARTERS = 4
Q_SPLIT = ((0, 6), (6, 12), (12, 18), (18, 22))
OUT_CHUNKS = QUARTERS * len(Q_SPLIT)
FFN_CHUNKS = IN_CHUNKS + OUT_CHUNKS
A_UNITS = 10
A_CHUNKS = A_UNITS + 4
FFN_BASE = (0, FFN_CHUNKS + A_CHUNKS, 2 * FFN_CHUNKS + A_CHUNKS, 3 * FFN_CHUNKS + A_CHUNKS + 1)
A_BASE = FFN_CHUNKS
C_BASE = 3 * FFN_CHUNKS + A_CHUNKS
CHUNKS = C_BASE + 1 + FFN_CHUNKS

SPLIT_NORMS = (0, 1, 2, 3, 5)
FFN_NORM = (0, 2, 3, 5)
NEXT_NORM = (1, 3, 4, 6)

SUM_STEPS = KD - 1

SUM_BANK, STAT_BANK, R_BANK = 3, 4, 2
A_OUT_BANK = (3, 0, 1, 2, 4, 5, 6, 7)
LN_BANK = (4, 5, 7, 4)

PC_G, PC_WA, PC_BA, PC_LG, PC_LB, PC_WB, PC_PB, PC_PS = 0, 56, 180, 184, 188, 192, 204, 212
PARAMS = 220


def out_bank(m):
    return 4 + m % 4


def build(nc, a):
    ctx = ExitStack()
    with ctx:
        def sb(name, shape, dt=F32):
            return ctx.enter_context(nc.sbuf_tensor(name, shape, dt))

        def sem(name):
            return ctx.enter_context(nc.semaphore(name))

        w_raw = sb("w_raw", [P, RING, SLOT])
        w_hi = sb("w_hi", [P, RING, SLOT], F32R)
        w_lo = sb("w_lo", [P, RING, SLOT], F32R)
        x = sb("x", [P, KD, T])
        x_hi = sb("x_hi", [P, KD, T], F32R)
        x_lo = sb("x_lo", [P, KD, T], F32R)
        h_hi = sb("h_hi", [P, KF, T], F32R)
        h_lo = sb("h_lo", [P, KF, T], F32R)
        scaled = sb("scaled", [P, 2, T])
        acted = sb("acted", [P, 2, T])
        norm_buf = sb("norm_buf", [P, 4, T])
        squares, rms, square_sum = norm_buf[:, 0:2, :], norm_buf[:, 2, :], norm_buf[:, 3, :]
        r = sb("r", [P, T])
        ones = sb("ones", [P, P])
        eps = sb("eps", [P, 1])
        primed = sb("primed", [P, 1])
        par = sb("par_sb", [P, PARAMS])
        bias_scaled = sb("bias_scaled", [P, KD])
        count_i = sb("count_i", [P, HC], mybir.dt.int32)
        inv_count = sb("inv_count", [P, len(WINDOWS), HC])
        head = sb("head", [P, 2, HC])
        mix = sb("mix", [P, 5760])
        psum = ctx.enter_context(nc.psum_tensor("psum", [P, 8, 512], F32))

        ea_w, eb_w = HA + PROMPT + SEQS * (HA + STEP), HB + PROMPT + SEQS * (HB + STEP)
        ext_a = mix[:, 0:KA * ea_w].rearrange("p (i n) -> p i n", i=KA)
        eb0 = KA * ea_w
        ext_b = mix[:, eb0:eb0 + KA * eb_w].rearrange("p (i n) -> p i n", i=KA)
        y0 = eb0 + KA * eb_w
        y_a = mix[:, y0:y0 + KA * T].rearrange("p (i n) -> p i n", i=KA)
        y_b = mix[:, y0 + KA * T:y0 + 2 * KA * T].rearrange("p (i n) -> p i n", i=KA)
        ln_sq = y_b
        n_prod = SEQS * STEP * TAPS_A
        tap_prod = norm_buf[:, :, :].rearrange("p a b -> p (a b)")[:, 0:n_prod].rearrange(
            "p (s t k) -> p s t k", s=SEQS, t=STEP)
        ec_w = HC + PROMPT + SEQS * (HC + STEP)
        ext_c = mix[:, 0:KD * ec_w].rearrange("p (i n) -> p i n", i=KD)
        win = [mix[:, (KD + 2 * z) * ec_w:(KD + 2 * z + 2) * ec_w].rearrange("p (i n) -> p i n", i=2)
               for z in range(2)]
        y_out = mix[:, 0:KD * T].rearrange("p (i n) -> p i n", i=KD)

        def prompt_of(ext, i, hist, at, n=PROMPT):
            return ext[:, i, at:at + n]

        def sample_of(ext, i, hist, at, n=STEP):
            s = ext[:, i, hist + PROMPT:hist + PROMPT + SEQS * (hist + STEP)]
            return s.rearrange("p (s n) -> p s n", s=SEQS)[:, :, at:at + n]

        def bank(b, lo=0, hi=T):
            return psum[:, b, lo:hi]

        def sample_cols(ap):
            return ap.rearrange("p (s n) -> p s n", s=SEQS)

        def pcol(c):
            return par[:, c:c + 1]

        w_landed = [sem(f"w_landed{i}") for i in range(RING)]
        w_high = sem("w_high")
        w_low = sem("w_low")
        w_used = sem("w_used")
        x_landed = sem("x_landed")
        par_landed = sem("par_landed")
        hist_ab_landed = sem("hist_ab_landed")
        hist_c_landed = sem("hist_c_landed")
        consts_set = sem("consts_set")
        pads_set = sem("pads_set")
        count_set = sem("count_set")
        x_new = sem("x_new")
        xg_ready = sem("xg_ready")
        x_high = sem("x_high")
        x_low = sem("x_low")
        squared = sem("squared")
        sum_step = sem("sum_step")
        stat_full = sem("stat_full")
        rms_ready = sem("rms_ready")
        r_ready = sem("r_ready")
        pair_full = sem("pair_full")
        gate_scaled = sem("gate_scaled")
        up_scaled = sem("up_scaled")
        gate_acted = sem("gate_acted")
        hid_ready = sem("hid_ready")
        hid_high = sem("hid_high")
        hid_low = sem("hid_low")
        a_gate_scaled = sem("a_gate_scaled")
        a_gate_acted = sem("a_gate_acted")
        a_evacuated = sem("a_evacuated")
        conv_prompt = sem("conv_prompt")
        tap_products = sem("tap_products")
        conv_sample_sum = sem("conv_sample_sum")
        conv_sample = sem("conv_sample")
        x_biased = sem("x_biased")
        prime_done = sem("prime_done")
        y_ready = sem("y_ready")
        y_high = sem("y_high")
        y_low = sem("y_low")
        ln_sum_full = sem("ln_sum_full")
        ln_centred = sem("ln_centred")
        ln_squared = sem("ln_squared")
        ln_var_full = sem("ln_var_full")
        ln_std_ready = sem("ln_std_ready")
        ln_scaled = sem("ln_scaled")
        a_out_full = sem("a_out_full")
        a_state_out = sem("a_state_out")
        c_h_ready = sem("c_h_ready")
        pooled_ready = sem("pooled_ready")
        pooled_high = sem("pooled_high")
        pooled_low = sem("pooled_low")
        c_out_full = sem("c_out_full")
        c_state_out = sem("c_state_out")
        y_done = sem("y_done")
        out_stored = sem("out_stored")
        own = sem("own")

        block = ctx.enter_context(nc.Block())

        def x_low_count(n, tiles):
            return KD * SPLIT_NORMS.index(n) + tiles

        def x_new_count(n, tiles):
            return KD * (n - 1) + tiles

        @block.sync
        def _(sp):
            def slot_free(c, more=0):
                sp.wait_ge(w_low, c - RING + 1 + more)

            def load(c, dst0, src0, dst1, src1):
                sp.dma_start(dst0, src0).then_inc(w_landed[c % RING], 16)
                sp.dma_start(dst1, src1).then_inc(w_landed[c % RING], 16)

            def load_in(f, c, half, unit):
                w = a["ffn_w_in"][f // 2, f % 2].rearrange("(k p) (g n) -> p k g n", p=P, g=2)
                dst = w_raw[:, c % RING, :].rearrange("p (k g n) -> p k g n", k=4, g=2)
                k = slice(4 * half, 4 * half + 4)
                cols = bass.ds(unit * 2 * P, 2 * P)
                load(c, dst[:, :, 0, :], w[:, k, 0, cols], dst[:, :, 1, :], w[:, k, 1, cols])

            def load_out(f, c, part, quarter):
                w = a["ffn_w_out"][f // 2, f % 2].rearrange("(k p) n -> p k n", p=P)
                k0, k1 = Q_SPLIT[part]
                km = (k0 + k1) // 2
                dst = w_raw[:, c % RING, 0:(k1 - k0) * 2 * P].rearrange("p (k n) -> p k n", n=2 * P)
                cols = bass.ds(quarter * 2 * P, 2 * P)
                load(c, dst[:, 0:km - k0, :], w[:, k0:km, cols], dst[:, km - k0:k1 - k0, :], w[:, km:k1, cols])

            def ffn(f):
                base = FFN_BASE[f]
                for j in range(RING):
                    if f > 0:
                        slot_free(base + j)
                    load_in(f, base + j, j % 2, j // 2)
                with sp.Fori(0, UNITS // 2 - 1) as i:
                    for j in range(RING, 2 * RING):
                        slot_free(base + j, 4 * i)
                        load_in(f, base + j, j % 2, 2 * i + j // 2)
                for j in range(4 * (UNITS // 2), IN_CHUNKS):
                    slot_free(base + j)
                    load_in(f, base + j, j % 2, j // 2)
                base += IN_CHUNKS
                with sp.Fori(0, QUARTERS) as q:
                    for j in range(RING):
                        slot_free(base + j, 4 * q)
                        load_out(f, base + j, j, q)

            def mixer_a():
                w = a["mix_w_in"][0].rearrange("(k p) n -> p k n", p=P)
                for v in range(A_UNITS):
                    c = A_BASE + v
                    slot_free(c)
                    dst = w_raw[:, c % RING, :].rearrange("p (k g n) -> p k g n", k=KD, g=2)
                    if v < 2 * KA:
                        c0 = (0 if v < KA else 3 * DA) + v % KA * P
                        load(c, dst[:, :, 0, :], w[:, :, c0:c0 + P], dst[:, :, 1, :], w[:, :, c0 + DA:c0 + DA + P])
                    else:
                        c0 = 2 * DA + (v - 2 * KA) * 2 * P
                        dst = w_raw[:, c % RING, :].rearrange("p (k n) -> p k n", k=KD)
                        load(c, dst[:, 0:4, :], w[:, 0:4, c0:c0 + 2 * P], dst[:, 4:8, :], w[:, 4:8, c0:c0 + 2 * P])
                w = a["mix_w_out"][0].rearrange("(k p) n -> p k n", p=P)
                for o in range(4):
                    c = A_BASE + A_UNITS + o
                    slot_free(c)
                    k0, c0 = (KA, 0)[o % 2], o // 2 * 512
                    dst = w_raw[:, c % RING, :].rearrange("p (k n) -> p k n", k=KA)
                    load(c, dst[:, 0:2, :], w[:, k0:k0 + 2, c0:c0 + 512],
                         dst[:, 2:4, :], w[:, k0 + 2:k0 + 4, c0:c0 + 512])

            def mixer_c():
                slot_free(C_BASE)
                w = a["pool_w"][0].rearrange("g (k p) n -> p (g k) n", p=P)
                dst = w_raw[:, C_BASE % RING, :].rearrange("p (k n) -> p k n", k=KD)
                load(C_BASE, dst[:, 0:4, :], w[:, 0:4, :], dst[:, 4:8, :], w[:, 4:8, :])

            ffn(0)
            mixer_a()
            ffn(1)
            ffn(2)
            mixer_c()
            ffn(3)
            for m in range(0, KD, 2):
                sp.wait_ge(y_done, m + 2)
                sp.dma_start(a["y_t"][:, m:m + 2, :], y_out[:, m:m + 2, :]).then_inc(out_stored, 16)
            sp.wait_ge(out_stored, 16 * KD // 2)

        @block.gpsimd
        def _(pool):
            pool.memset(ones[:, :], 1.0)
            pool.memset(eps[:, :], EPS).then_inc(consts_set, 1)
            pool.memset(ext_a[:, :, 0:HA], 0.0)
            pool.memset(ext_b[:, :, 0:HB], 0.0).then_inc(pads_set, 1)
            pool.iota(count_i[:, :], pattern=[[1, HC]], base=1, channel_multiplier=0).then_inc(count_set, 1)

            def low(c, n, more=0):
                pool.wait_ge(w_high, c + 1 + more)
                s = c % RING
                pool.tensor_tensor(w_lo[:, s, 0:n], w_raw[:, s, 0:n], w_hi[:, s, 0:n].bitcast(F32),
                                   ALU.subtract).then_inc(w_low, 1)

            def ffn(f):
                base = FFN_BASE[f]
                with pool.Fori(0, UNITS // 2) as i:
                    for j in range(RING):
                        low(base + j, SLOT, 4 * i)
                for j in range(4 * (UNITS // 2), IN_CHUNKS):
                    low(base + j, SLOT)
                base += IN_CHUNKS
                with pool.Fori(0, QUARTERS) as q:
                    for j in range(RING):
                        low(base + j, (Q_SPLIT[j][1] - Q_SPLIT[j][0]) * 2 * P, 4 * q)

            def tap_product(i):
                pool.wait_ge(a_evacuated, i + 1)
                if i == 0:
                    pool.wait_ge(par_landed, 16)
                    pool.wait_ge(hist_ab_landed, 16 * 2 * KA)
                else:
                    pool.wait_ge(conv_sample_sum, i)
                row = sample_of(ext_a, i, HA, 0)
                under = bass.AP(row.tensor, row.offset, [[5760, P], [HA + STEP, SEQS], [1, STEP], [1, TAPS_A]])
                taps = par[:, PC_WA + TAPS_A * i:PC_WA + TAPS_A * (i + 1)]
                taps = taps.unsqueeze(1).unsqueeze(1).broadcast_to([P, SEQS, STEP, TAPS_A])
                pool.tensor_tensor(tap_prod, under, taps, ALU.mult).then_inc(tap_products, 1)

            ffn(0)
            for c in range(A_BASE, A_BASE + A_CHUNKS):
                low(c, SLOT)
                i = c - A_BASE - PRODUCTS_LAG
                if 0 <= i < KA:
                    tap_product(i)
            ffn(1)
            ffn(2)
            low(C_BASE, SLOT)
            ffn(3)

        def chunk_cols(c):
            for base in FFN_BASE:
                if base + IN_CHUNKS <= c < base + FFN_CHUNKS:
                    k0, k1 = Q_SPLIT[(c - base - IN_CHUNKS) % 4]
                    return (k1 - k0) * 2 * P
            return SLOT

        @block.scalar
        def _(act):
            def high(c, i=None):
                if c >= CHUNKS:
                    return
                more = 0 if i is None else i
                n = chunk_cols(c)
                act.wait_ge(w_landed[c % RING], 32 * (c // RING + 1) + 32 * more)
                if c >= RING:
                    act.wait_ge(w_used, c - RING + 1 + RING * more)
                act.activation(w_hi[:, c % RING, 0:n], w_raw[:, c % RING, 0:n], ACT.Copy).then_inc(w_high, 1)

            def norm_tile(n, m):
                if n == 5:
                    act.wait_ge(x_new, x_new_count(n, m + 1))
                    act.activation(x_hi[:, m, :], x[:, m, :], ACT.Copy,
                                   scale=pcol(PC_G + KD * n + m)).then_inc(x_high, 1)
                elif n in SPLIT_NORMS:
                    act.wait_ge(xg_ready, x_low_count(n, m + 1))
                    b = A_OUT_BANK[m] if n == 2 else out_bank(m)
                    act.activation(x_hi[:, m, :], bank(b), ACT.Copy).then_inc(x_high, 1)
                if n == 0:
                    act.wait_ge(x_landed, 16)
                else:
                    act.wait_ge(x_new, x_new_count(n, m + 1))
                if m == 0 and n == 2:
                    act.wait_ge(x_low, x_low_count(n, 1))
                if m >= 3:
                    act.wait_ge(sum_step, SUM_STEPS * n + m - 2)
                dst = bank(SUM_BANK) if m == 0 else squares[:, m % 2, :]
                act.activation(dst, x[:, m, :], ACT.Square).then_inc(squared, 1)

            primes = [0]

            def prime(func):
                if primes[0]:
                    act.wait_ge(prime_done, primes[0])
                primes[0] += 1
                act.activation(primed[:, :], eps[:, :], func).then_inc(prime_done, 1)

            def root(n):
                act.wait_ge(stat_full, n + 1)
                act.activation(rms, bank(STAT_BANK), ACT.Sqrt, bias=eps[:, :],
                               scale=1.0 / D).then_inc(rms_ready, 1)

            def hidden(f, b, z, j, pairs_before):
                act.wait_ge(gate_scaled, pairs_before + 1)
                act.activation(acted[:, z, :], scaled[:, z, :], ACT.Silu).then_inc(gate_acted, 1)
                act.wait_ge(hid_ready, pairs_before + 1)
                act.activation(h_hi[:, j, :], bank(b), ACT.Copy).then_inc(hid_high, 1)

            def hidden_at(f, p, i=None):
                b = 4 * (p // 2 % 2) + 2 * (p % 2)
                if i is None:
                    hidden(f, b, p % 2, p, KF * f + p)
                else:
                    hidden(f, b, p % 2, bass.ds(4 * i + p, 1), 4 * i + (KF * f + p))

            def ffn(f):
                base = FFN_BASE[f]
                root(FFN_NORM[f])
                prime(ACT.Silu)
                high(base + RING)
                high(base + RING + 1)
                hidden_at(f, 0)
                hidden_at(f, 1)
                for p in range(2, 4):
                    high(base + RING + p)
                    hidden_at(f, p)
                with act.Fori(0, 3) as i:
                    for p in range(4, 8):
                        high(base + RING + p, i)
                        hidden_at(f, p, i)
                for p in range(16, IN_CHUNKS):
                    high(base + RING + p)
                    hidden_at(f, p)
                base += IN_CHUNKS
                prime(ACT.Sqrt)
                for q in range(QUARTERS):
                    for j in range(3):
                        high(base + 4 * q + j + RING)
                    for m in (2 * q, 2 * q + 1):
                        norm_tile(NEXT_NORM[f], m)
                    if q == QUARTERS - 1 and NEXT_NORM[f] not in SPLIT_NORMS:
                        root(NEXT_NORM[f])
                    high(base + 4 * q + 3 + RING)

            def split_y(k, b):
                act.activation(h_hi[:, k, :], bank(b), ACT.Copy).then_inc(y_high, 1)

            def mixer_a():
                root(1)
                prime(ACT.Sigmoid)
                high(A_BASE + RING)
                for v in range(A_UNITS):
                    if v > 0:
                        high(A_BASE + RING + v)
                    if v < KA:
                        act.wait_ge(a_gate_scaled, v + 1)
                        act.activation(acted[:, v % 2, :], scaled[:, v % 2, :], ACT.Sigmoid).then_inc(a_gate_acted, 1)
                    elif v >= 2 * KA:
                        for t in range(2):
                            i = 2 * (v - 2 * KA) + t
                            act.wait_ge(y_ready, i + 1)
                            split_y(KA + i, 2 * (v % 2) + t)
                prime(ACT.Sqrt)
                for i in range(KA):
                    act.wait_ge(ln_centred, i + 1)
                    act.activation(ln_sq[:, i, :], y_a[:, i, :], ACT.Square).then_inc(ln_squared, 1)
                act.wait_ge(ln_var_full, 1)
                act.activation(rms, bank(5), ACT.Sqrt, bias=eps[:, :], scale=1.0 / DA).then_inc(ln_std_ready, 1)
                prime(ACT.Silu)
                for i in range(KA):
                    act.wait_ge(ln_scaled, i + 1)
                    if i == 3:
                        act.wait_ge(y_low, KA + 1)
                    act.activation(bank(LN_BANK[i]), y_a[:, i, :], ACT.Silu, bias=pcol(PC_LB + i),
                                   scale=pcol(PC_LG + i)).then_inc(y_ready, 1)
                    act.wait_ge(y_ready, KA + i + 1)
                    split_y(i, LN_BANK[i])
                prime(ACT.Sqrt)
                high(A_BASE + A_UNITS + RING)
                high(A_BASE + A_UNITS + 1 + RING)
                for m in range(KA):
                    norm_tile(2, m)
                high(A_BASE + A_UNITS + 2 + RING)
                for m in range(KA, KD - 1):
                    norm_tile(2, m)
                norm_tile(2, KD - 1)
                high(A_BASE + A_UNITS + 3 + RING)

            def mixer_a_state():
                act.wait_ge(a_evacuated, 2 * KA)
                act.wait_ge(hist_ab_landed, 16 * 2 * KA)
                for i in range(KA):
                    act.dma_start(a["new_a_prompt"][:, i, :], ext_a[:, i, PROMPT:PROMPT + HA]).then_inc(a_state_out, 16)
                    act.dma_start(a["new_a_sample"][:, i, :, :], sample_of(ext_a, i, HA, STEP, HA)).then_inc(a_state_out, 16)
                    act.dma_start(a["new_b_prompt"][:, i, :], ext_b[:, i, PROMPT:PROMPT + HB]).then_inc(a_state_out, 16)
                    act.dma_start(a["new_b_sample"][:, i, :, :], sample_of(ext_b, i, HB, STEP, HB)).then_inc(a_state_out, 16)

            def mixer_c_history():
                act.wait_ge(a_state_out, 16 * 4 * KA)
                act.wait_ge(y_low, KD)
                for m in range(KD):
                    act.dma_start(sample_of(ext_c, m, HC, 0, HC), a["hist_c"][:, m, :, :]).then_inc(hist_c_landed, 16)

            def mixer_c():
                for g in range(4):
                    tiles = (2 * g, 2 * g + 1)
                    for m in tiles:
                        act.wait_ge(c_h_ready, m + 1)
                        act.activation(x[:, m, :], x[:, m, :], ACT.Identity,
                                       bias=bias_scaled[:, m:m + 1]).then_inc(x_biased, 1)
                    if g > 1:
                        norm_tile(5, 2 * g - 4)
                        norm_tile(5, 2 * g - 3)
                    for m in tiles:
                        act.wait_ge(pooled_ready, m + 1)
                        act.activation(h_hi[:, m, :], bank(m % 2), ACT.Copy).then_inc(pooled_high, 1)
                for m in range(KD - 4, KD):
                    norm_tile(5, m)
                high(C_BASE + RING)

            def mixer_c_state():
                act.wait_ge(c_h_ready, KD)
                for m in range(KD):
                    act.dma_start(a["new_c_prompt"][:, m, :], ext_c[:, m, PROMPT:PROMPT + HC]).then_inc(c_state_out, 16)
                    act.dma_start(a["new_c_sample"][:, m, :, :], sample_of(ext_c, m, HC, STEP, HC)).then_inc(c_state_out, 16)

            act.dma_start(x[:, :, :], a["x_t"]).then_inc(x_landed, 16)
            act.dma_start(par[:, :], a["par"]).then_inc(par_landed, 16)
            for i in range(KA):
                act.dma_start(sample_of(ext_a, i, HA, 0, HA), a["hist_a"][:, i, :, :]).then_inc(hist_ab_landed, 16)
                act.dma_start(sample_of(ext_b, i, HB, 0, HB), a["hist_b"][:, i, :, :]).then_inc(hist_ab_landed, 16)
            act.wait_ge(consts_set, 1)
            high(0)
            for m in range(4):
                norm_tile(0, m)
            high(1)
            for m in range(4, KD):
                norm_tile(0, m)
            high(2)
            high(3)
            ffn(0)
            mixer_a()
            mixer_a_state()
            ffn(1)
            mixer_c_history()
            ffn(2)
            mixer_c()
            mixer_c_state()
            ffn(3)
            act.wait_ge(c_state_out, 16 * 2 * KD)

        @block.tensor
        def _(pe):
            def product(b, s, col, hi, lo, k, first, last):
                w_h, w_l = w_hi[:, s, col:col + P], w_lo[:, s, col:col + P]
                pe.matmul(bank(b), w_h, hi[:, k, :], start=first, stop=False)
                pe.matmul(bank(b), w_h, lo[:, k, :], start=False, stop=False)
                return pe.matmul(bank(b), w_l, hi[:, k, :], start=False, stop=last)

            def stat(n):
                pe.wait_ge(sum_step, SUM_STEPS * (n + 1))
                pe.matmul(bank(STAT_BANK), ones[:, :], square_sum, start=True, stop=True).then_inc(stat_full, 1)

            def unit_half(c, banks, half, more=0, before_last=None):
                pe.wait_ge(w_low, c + 1 + more)
                for z in range(4):
                    g, pair = z % 2, z // 2
                    if z == 3 and before_last is not None:
                        before_last()
                    for k in range(4):
                        mm = product(banks + z, c % RING, (2 * k + g) * 2 * P + pair * P, x_hi, x_lo, 4 * half + k,
                                     half == 0 and k == 0, half == 1 and k == 3)
                    if half == 1 and z == 1:
                        mm.then_inc(pair_full, 1)
                mm.then_inc(w_used, 1)

            def ffn(f):
                base, n = FFN_BASE[f], FFN_NORM[f]
                pe.wait_ge(x_low, x_low_count(n, 4))
                unit_half(base, 0, 0, before_last=lambda: pe.wait_ge(sum_step, SUM_STEPS * (n + 1)))
                pe.wait_ge(x_low, x_low_count(n, KD))
                stat(n)
                unit_half(base + 1, 0, 1)
                pe.wait_ge(r_ready, n + 1)
                unit_half(base + 2, 4, 0)
                unit_half(base + 3, 4, 1)
                with pe.Fori(0, UNITS // 2 - 1) as i:
                    for j in range(4, 8):
                        if j % 2 == 0:
                            pe.wait_ge(hid_low, 4 * i + (KF * f + j - 2))
                        unit_half(base + j, 4 * (j // 2 % 2), j % 2, 4 * i)
                pe.wait_ge(hid_low, KF * f + 2 * (UNITS - 2))
                unit_half(base + IN_CHUNKS - 2, 0, 0)
                unit_half(base + IN_CHUNKS - 1, 0, 1)
                base += IN_CHUNKS
                pe.wait_ge(hid_low, KF * f + 2 * (UNITS - 1))
                nn = NEXT_NORM[f]
                with pe.Fori(0, QUARTERS // 2) as i:
                    for q in range(2):
                        if nn in SPLIT_NORMS:
                            pe.wait_ge(x_low, 4 * i + x_low_count(nn, 2 * q - 2))
                        else:
                            pe.wait_ge(x_new, 4 * i + x_new_count(nn, 2 * q - 2))
                        for part, (k0, k1) in enumerate(Q_SPLIT):
                            c = base + 4 * q + part
                            pe.wait_ge(w_low, 8 * i + c + 1)
                            if q == 0 and part == 3:
                                pe.wait_ge(hid_low, KF * (f + 1))
                            for z in range(2):
                                for k in range(k0, k1):
                                    mm = product(4 + 2 * q + z, c % RING, (k - k0) * 2 * P + z * P, h_hi, h_lo, k,
                                                 k == 0, k == KF - 1)
                            mm.then_inc(w_used, 1)

            def mixer_a():
                for v in range(A_UNITS):
                    c = A_BASE + v
                    banks = 2 * (v % 2)
                    if v == 1:
                        stat(1)
                    if v >= 2:
                        pe.wait_ge(a_evacuated, v - 1)
                    pe.wait_ge(w_low, c + 1)
                    for k in range(KD):
                        if v == 0:
                            pe.wait_ge(x_low, x_low_count(1, k + 1))
                        for z in range(2):
                            mm = product(banks + z, c % RING, (2 * k + z) * P, x_hi, x_lo, k, k == 0, k == KD - 1)
                    mm.then_inc(w_used, 1)
                base = A_BASE + A_UNITS

                def late_part(c):
                    for k in range(KA):
                        pe.wait_ge(y_low, KA + k + 1)
                        for m in range(KA):
                            mm = product(A_OUT_BANK[m], c % RING, k * 512 + m * P, h_hi, h_lo, k, False, k == KA - 1)
                            if k == KA - 1:
                                mm.then_inc(a_out_full if m < KA - 1 else w_used, 1)

                def part(c, tiles, k_base, first, whole=True):
                    for m in tiles:
                        for k in range(KA):
                            mm = product(A_OUT_BANK[m], c % RING, k * 512 + m % 4 * P, h_hi, h_lo, k_base + k,
                                         first and k == 0, not first and k == KA - 1)
                        if not first and m % 4 < 3:
                            mm.then_inc(a_out_full, 1)
                    if whole:
                        mm.then_inc(w_used, 1)

                for i in range(KA):
                    pe.wait_ge(conv_prompt, TAPS_A * (i + 1))
                    pe.wait_ge(conv_sample, i + 1)
                    mm = pe.matmul(bank(4), ones[:, :], y_a[:, i, :], start=i == 0, stop=i == KA - 1)
                mm.then_inc(ln_sum_full, 1)
                pe.wait_ge(y_low, KA)
                pe.wait_ge(w_low, base + 1)
                part(base, (0, 1), KA, True, whole=False)
                for i in range(KA):
                    pe.wait_ge(ln_squared, i + 1)
                    mm = pe.matmul(bank(5), ones[:, :], ln_sq[:, i, :], start=i == 0, stop=i == KA - 1)
                mm.then_inc(ln_var_full, 1)
                part(base, (2, 3), KA, True)
                pe.wait_ge(w_low, base + 2)
                late_part(base + 1)
                pe.wait_ge(w_low, base + 3)
                part(base + 2, range(KA, KD), KA, True)
                pe.wait_ge(w_low, base + 4)
                part(base + 3, range(KA, KD), 0, False)

            def mixer_c():
                stat(4)
                pe.wait_ge(w_low, C_BASE + 1)
                for g in range(4):
                    pe.wait_ge(pooled_low, 2 * g + 2)
                    if g >= 2:
                        pe.wait_ge(x_low, x_low_count(5, 2 * g - 2))
                    for z in range(2):
                        for k in range(2):
                            mm = product(out_bank(2 * g + z), C_BASE % RING, (2 * g + k) * 2 * P + z * P, h_hi, h_lo,
                                         2 * g + k, k == 0, k == 1)
                    mm.then_inc(c_out_full if g < 3 else w_used, 1)

            ffn(0)
            mixer_a()
            ffn(1)
            ffn(2)
            mixer_c()
            ffn(3)
            stat(6)

        @block.vector
        def _(dve):
            steps = [0]

            def mark(ins):
                steps[0] += 1
                ins.then_inc(own, 1)

            def settle():
                dve.wait_ge(own, steps[0])

            def xg(n, m):
                b = A_OUT_BANK[m] if n == 2 else out_bank(m)
                if n > 0:
                    dve.wait_ge(x_new, x_new_count(n, m + 1))
                elif m >= 4:
                    dve.wait_ge(x_low, m - 3)
                dve.tensor_scalar(bank(b), x[:, m, :], pcol(PC_G + KD * n + m), None, ALU.mult).then_inc(xg_ready, 1)

            def close_tile(n, m):
                if n == 5:
                    dve.wait_ge(x_high, x_low_count(n, m + 1))
                    dve.scalar_tensor_tensor(out=x_lo[:, m, :], in0=x[:, m, :], scalar=pcol(PC_G + KD * n + m),
                                             in1=x_hi[:, m, :].bitcast(F32), op0=ALU.mult,
                                             op1=ALU.subtract).then_inc(x_low, 1)
                elif n in SPLIT_NORMS:
                    b = A_OUT_BANK[m] if n == 2 else out_bank(m)
                    dve.wait_ge(x_high, x_low_count(n, m + 1))
                    dve.tensor_tensor(x_lo[:, m, :], bank(b), x_hi[:, m, :].bitcast(F32), ALU.subtract).then_inc(x_low, 1)
                if m > 0:
                    dve.wait_ge(squared, KD * n + m + 1)
                    if m > 1:
                        dve.wait_ge(sum_step, SUM_STEPS * n + m - 1)
                    dst = square_sum if m == KD - 1 else bank(SUM_BANK)
                    dve.tensor_tensor(dst, bank(SUM_BANK), squares[:, m % 2, :], ALU.add).then_inc(sum_step, 1)

            def inverse(n, dst):
                dve.wait_ge(rms_ready, n + 1)
                dve.reciprocal(dst, rms).then_inc(r_ready, 1)
                dve.wait_ge(r_ready, n + 1)

            def hidden(f, p, i=0):
                b, z, count = 2 * (p % 4), p % 2, 4 * i + (KF * f + p + 1)
                j = p if isinstance(i, int) else bass.ds(4 * i + p, 1)
                if p % 2 == 0:
                    dve.wait_ge(pair_full, 2 * i + (UNITS * f + p // 2 + 1))
                else:
                    dve.wait_ge(w_used, 4 * i + (FFN_BASE[f] + p + 1))
                dve.tensor_tensor(scaled[:, z, :], bank(b), r[:, :], ALU.mult).then_inc(gate_scaled, 1)
                dve.tensor_tensor(bank(b + 1), bank(b + 1), r[:, :], ALU.mult).then_inc(up_scaled, 1)
                dve.wait_ge(gate_acted, count)
                dve.wait_ge(up_scaled, count)
                dve.tensor_tensor(bank(b), bank(b + 1), acted[:, z, :], ALU.mult).then_inc(hid_ready, 1)
                dve.wait_ge(hid_high, count)
                dve.tensor_tensor(h_lo[:, j, :], bank(b), h_hi[:, j, :].bitcast(F32), ALU.subtract).then_inc(hid_low, 1)

            def ffn(f):
                inverse(FFN_NORM[f], r[:, :])
                with dve.Fori(0, UNITS // 2) as i:
                    for p in range(4):
                        hidden(f, p, i)
                for p in range(4 * (UNITS // 2), KF):
                    hidden(f, p)
                n = NEXT_NORM[f]
                for q in range(QUARTERS):
                    dve.wait_ge(w_used, FFN_BASE[f] + IN_CHUNKS + 4 * (q + 1))
                    for m in (2 * q, 2 * q + 1):
                        dve.scalar_tensor_tensor(out=x[:, m, :], in0=bank(out_bank(m)), scalar=0.5, in1=x[:, m, :],
                                                 op0=ALU.mult, op1=ALU.add).then_inc(x_new, 1)
                        if n in SPLIT_NORMS:
                            xg(n, m)
                    close_tile(n, 2 * q)
                    close_tile(n, 2 * q + 1)

            def glu(v):
                b = 2 * (v % 2)
                dve.wait_ge(w_used, A_BASE + v + 1)
                dve.tensor_tensor(scaled[:, v % 2, :], bank(b + 1), r[:, :], ALU.mult).then_inc(a_gate_scaled, 1)
                mark(dve.tensor_tensor(bank(b), bank(b), r[:, :], ALU.mult))
                dve.wait_ge(a_gate_acted, v + 1)
                settle()
                mark(dve.tensor_tensor(prompt_of(ext_a, v, HA, HA), bank(b, 0, PROMPT), acted[:, v % 2, 0:PROMPT],
                                       ALU.mult))
                dve.tensor_tensor(sample_of(ext_a, v, HA, HA), sample_cols(bank(b, PROMPT, T)),
                                  sample_cols(acted[:, v % 2, PROMPT:T]), ALU.mult).then_inc(a_evacuated, 1)

            def tap_a(i, k):
                n = TAPS_A * i + k
                w = pcol(PC_WA + TAPS_A * i + k)
                src, acc = prompt_of(ext_a, i, HA, k), bank(4 + i, 0, PROMPT)
                if k == 0:
                    dve.tensor_scalar(acc, src, w, pcol(PC_BA + i), ALU.mult, ALU.add).then_inc(conv_prompt, 1)
                else:
                    dve.wait_ge(conv_prompt, n)
                    dve.scalar_tensor_tensor(out=y_a[:, i, 0:PROMPT] if k == TAPS_A - 1 else acc, in0=src, scalar=w,
                                             in1=acc, op0=ALU.mult, op1=ALU.add).then_inc(conv_prompt, 1)

            def sum_taps(i):
                dve.wait_ge(tap_products, i + 1)
                res = y_a[:, i, PROMPT:T]
                dve.tensor_reduce(sample_cols(res), tap_prod, mybir.AxisListType.X, ALU.add).then_inc(conv_sample_sum, 1)
                dve.wait_ge(conv_sample_sum, i + 1)
                dve.tensor_scalar(res, res, pcol(PC_BA + i), None, ALU.add).then_inc(conv_sample, 1)

            def conv_b(v):
                i, b = v - KA, 2 * (v % 2)
                dve.wait_ge(w_used, A_BASE + v + 1)
                mark(dve.tensor_tensor(scaled[:, v % 2, :], bank(b), r[:, :], ALU.mult))
                mark(dve.tensor_tensor(bank(b + 1), bank(b + 1), r[:, :], ALU.mult))
                settle()
                mark(dve.tensor_tensor(prompt_of(ext_b, i, HB, HB), bank(b + 1, 0, PROMPT), scaled[:, v % 2, 0:PROMPT],
                                       ALU.mult))
                mark(dve.tensor_tensor(sample_of(ext_b, i, HB, HB), sample_cols(bank(b + 1, PROMPT, T)),
                                       sample_cols(scaled[:, v % 2, PROMPT:T]), ALU.mult))
                last = sample_cols(bank(b + 1, PROMPT, T))
                for k in range(TAPS_B):
                    settle()
                    w = pcol(PC_WB + TAPS_B * i + k)
                    for src, acc, res in (
                            (prompt_of(ext_b, i, HB, k), bank(b + 1, 0, PROMPT), y_b[:, i, 0:PROMPT]),
                            (sample_of(ext_b, i, HB, k), last,
                             sample_cols(y_b[:, i, PROMPT:T]))):
                        if k == 0:
                            ins = dve.tensor_scalar(acc, src, w, None, ALU.mult)
                        else:
                            ins = dve.scalar_tensor_tensor(out=res if k == TAPS_B - 1 else acc, in0=src, scalar=w,
                                                           in1=acc, op0=ALU.mult, op1=ALU.add)
                        if acc is not last or k < TAPS_B - 1:
                            mark(ins)
                ins.then_inc(a_evacuated, 1)

            def gate_b(v):
                dve.wait_ge(a_evacuated, 2 * KA)
                dve.wait_ge(w_used, A_BASE + v + 1)
                for t in range(2):
                    b, i = 2 * (v % 2) + t, 2 * (v - 2 * KA) + t
                    mark(dve.tensor_tensor(bank(b), bank(b), r[:, :], ALU.mult))
                    settle()
                    dve.tensor_tensor(bank(b), bank(b), y_b[:, i, :], ALU.mult).then_inc(y_ready, 1)
                for t in range(2):
                    b, i = 2 * (v % 2) + t, 2 * (v - 2 * KA) + t
                    dve.wait_ge(y_high, i + 1)
                    ins = dve.tensor_tensor(h_lo[:, KA + i, :], bank(b), h_hi[:, KA + i, :].bitcast(F32), ALU.subtract)
                    ins.then_inc(y_low, 1)

            def mixer_a():
                inverse(1, r[:, :])
                dve.wait_ge(pads_set, 1)
                dve.wait_ge(hist_ab_landed, 16 * 2 * KA)
                taps = [(i, k) for i in range(KA) for k in range(TAPS_A)]
                for v in range(A_UNITS):
                    (glu if v < KA else conv_b if v < 2 * KA else gate_b)(v)
                    if SUM_AT <= v < SUM_AT + KA:
                        sum_taps(v - SUM_AT)
                    for _ in range(TAPS_BETWEEN):
                        if taps and taps[0][0] <= v:
                            i, k = taps.pop(0)
                            if k == 0:
                                dve.wait_ge(a_evacuated, i + 1)
                                settle()
                            tap_a(i, k)
                for i, k in taps:
                    if k == 0:
                        dve.wait_ge(a_evacuated, i + 1)
                    tap_a(i, k)
                dve.wait_ge(ln_sum_full, 1)
                for i in range(KA):
                    dve.scalar_tensor_tensor(out=y_a[:, i, :], in0=bank(4), scalar=-1.0 / DA, in1=y_a[:, i, :],
                                             op0=ALU.mult, op1=ALU.add).then_inc(ln_centred, 1)
                dve.wait_ge(ln_std_ready, 1)
                mark(dve.reciprocal(bank(6), rms))
                settle()
                for i in range(KA):
                    dve.tensor_tensor(y_a[:, i, :], y_a[:, i, :], bank(6), ALU.mult).then_inc(ln_scaled, 1)
                for i in range(KA):
                    dve.wait_ge(y_high, KA + i + 1)
                    dve.tensor_tensor(h_lo[:, i, :], bank(LN_BANK[i]), h_hi[:, i, :].bitcast(F32),
                                      ALU.subtract).then_inc(y_low, 1)
                def add_out(m):
                    if m % 4 == 3:
                        dve.wait_ge(w_used, A_BASE + A_UNITS + m // 4 * 2 + 2)
                    else:
                        dve.wait_ge(a_out_full, 3 * (m // 4) + m % 4 + 1)
                    dve.tensor_tensor(x[:, m, :], bank(A_OUT_BANK[m]), x[:, m, :], ALU.add).then_inc(x_new, 1)
                    xg(2, m)
                for m in range(KD):
                    add_out(m)
                    if m > 0:
                        close_tile(2, m - 1)
                close_tile(2, KD - 1)

            def mixer_c():
                dve.wait_ge(a_state_out, 16 * 4 * KA)
                mark(dve.memset(ext_c[:, :, 0:HC], 0.0))
                dve.wait_ge(count_set, 1)
                mark(dve.tensor_copy(inv_count[:, 0, :], count_i[:, :]))
                settle()
                for g in (3, 2, 1, 0):
                    mark(dve.tensor_scalar(inv_count[:, g, :], inv_count[:, 0, :], float(WINDOWS[g]), None, ALU.min))
                settle()
                mark(dve.reciprocal(inv_count[:, :, :], inv_count[:, :, :]))
                mark(dve.tensor_tensor(bias_scaled[:, :], par[:, PC_PB:PC_PB + KD], par[:, PC_PS:PC_PS + KD], ALU.mult))
                inverse(4, bank(R_BANK))
                dve.wait_ge(hist_c_landed, 16 * KD)
                settle()

                def normalised(m):
                    g = pcol(PC_G + KD * 4 + m)
                    mark(dve.scalar_tensor_tensor(out=prompt_of(ext_c, m, HC, HC), in0=x[:, m, 0:PROMPT], scalar=g,
                                                  in1=bank(R_BANK, 0, PROMPT), op0=ALU.mult, op1=ALU.mult))
                    dve.scalar_tensor_tensor(out=sample_of(ext_c, m, HC, HC), in0=sample_cols(x[:, m, PROMPT:T]),
                                             scalar=g, in1=sample_cols(bank(R_BANK, PROMPT, T)), op0=ALU.mult,
                                             op1=ALU.mult).then_inc(c_h_ready, 1)

                def pooled_rest(g):
                    for m in (2 * g, 2 * g + 1):
                        dve.wait_ge(pooled_high, m + 1)
                        dve.tensor_tensor(h_lo[:, m, :], bank(m % 2), h_hi[:, m, :].bitcast(F32),
                                          ALU.subtract).then_inc(pooled_low, 1)

                def residual(g):
                    if g < 3:
                        dve.wait_ge(c_out_full, g + 1)
                    else:
                        dve.wait_ge(w_used, C_BASE + 1)
                    for m in (2 * g, 2 * g + 1):
                        dve.wait_ge(x_biased, m + 1)
                        dve.scalar_tensor_tensor(out=x[:, m, :], in0=bank(out_bank(m)), scalar=pcol(PC_PS + m),
                                                 in1=x[:, m, :], op0=ALU.mult, op1=ALU.add).then_inc(x_new, 1)
                    close_tile(5, 2 * g)
                    close_tile(5, 2 * g + 1)

                for g, w in enumerate(WINDOWS):
                    src, tile, n, z = ext_c, slice(2 * g, 2 * g + 2), 1, 0
                    normalised(2 * g)
                    normalised(2 * g + 1)
                    dve.wait_ge(c_h_ready, 2 * g + 2)
                    settle()
                    if g > 0:
                        dve.wait_ge(pooled_ready, 2 * g)
                    while n < w:
                        first = 2 * n - 1
                        mark(dve.tensor_tensor(win[z][:, :, first:ec_w], src[:, tile, first:ec_w],
                                               src[:, tile, first - n:ec_w - n], ALU.add))
                        settle()
                        src, tile, n, z = win[z], slice(0, 2), 2 * n, 1 - z
                    mark(dve.tensor_tensor(head[:, 0, :], src[:, 0, HC:2 * HC], inv_count[:, g, :], ALU.mult))
                    mark(dve.tensor_tensor(head[:, 1, :], src[:, 1, HC:2 * HC], inv_count[:, g, :], ALU.mult))
                    if g > 0:
                        pooled_rest(g - 1)
                        dve.wait_ge(pooled_low, 2 * g)
                    if g > 1:
                        residual(g - 2)
                    settle()
                    for m in (2 * g, 2 * g + 1):
                        b = m % 2
                        mark(dve.tensor_tensor(bank(b, 0, HC), head[:, b, :], ext_c[:, m, HC:2 * HC], ALU.subtract))
                        mark(dve.scalar_tensor_tensor(out=bank(b, HC, PROMPT), in0=src[:, b, 2 * HC:HC + PROMPT],
                                                      scalar=1.0 / w, in1=ext_c[:, m, 2 * HC:HC + PROMPT],
                                                      op0=ALU.mult, op1=ALU.subtract))
                        dve.scalar_tensor_tensor(out=sample_cols(bank(b, PROMPT, T)), in0=sample_of(src, b, HC, HC),
                                                 scalar=1.0 / w, in1=sample_of(ext_c, m, HC, HC),
                                                 op0=ALU.mult, op1=ALU.subtract).then_inc(pooled_ready, 1)
                pooled_rest(3)
                residual(2)
                residual(3)

            def final():
                inverse(6, bank(R_BANK))
                dve.wait_ge(c_state_out, 16 * 2 * KD)
                for m in range(KD):
                    dve.scalar_tensor_tensor(out=y_out[:, m, :], in0=x[:, m, :], scalar=pcol(PC_G + KD * 6 + m),
                                             in1=bank(R_BANK), op0=ALU.mult, op1=ALU.mult).then_inc(y_done, 1)

            dve.wait_ge(par_landed, 16)
            dve.wait_ge(x_landed, 16)
            for m in range(4):
                xg(0, m)
            for m in range(4):
                close_tile(0, m)
                xg(0, m + 4)
            for m in range(4, KD):
                close_tile(0, m)
            ffn(0)
            mixer_a()
            ffn(1)
            ffn(2)
            mixer_c()
            ffn(3)
            final()


TAPS_BETWEEN = 10
SUM_AT = 3
PRODUCTS_LAG = 4

INPUTS = {
    "x_t": (P, KD, T), "par": (P, PARAMS), "hist_a": (P, KA, SEQS, HA), "hist_b": (P, KA, SEQS, HB),
    "hist_c": (P, KD, SEQS, HC), "ffn_w_in": (2, 2, D, 2 * DFF), "ffn_w_out": (2, 2, DFF, D),
    "mix_w_in": (1, D, 5 * DA), "mix_w_out": (1, D, D), "pool_w": (1, 4, 256, 256),
}
OUTPUTS = {
    "y_t": (P, KD, T), "new_a_prompt": (P, KA, HA), "new_a_sample": (P, KA, SEQS, HA),
    "new_b_prompt": (P, KA, HB), "new_b_sample": (P, KA, SEQS, HB),
    "new_c_prompt": (P, KD, HC), "new_c_sample": (P, KD, SEQS, HC),
}


def kernel(**inputs):
    import numpy as np
    from concourse import bacc
    from concourse.bass_utils import run_bass_kernel_spmd

    g = {k: np.asarray(v) for k, v in inputs.items()}

    def by_partition(v):
        v = v.reshape(*v.shape[:-1], v.shape[-1] // P, P)
        return np.moveaxis(v, -1, 0)

    tokens = np.concatenate([g["x_prompt"].reshape(PROMPT, D), g["x_sample"].reshape(SEQS * STEP, D)])
    par = np.concatenate([
        by_partition(g["norm_g"]).reshape(P, 6 * KD),
        by_partition(g["final_norm_g"]),
        by_partition(g["conv_a_w"][0]).transpose(0, 2, 1).reshape(P, KA * TAPS_A),
        by_partition(g["conv_a_b"][0]), by_partition(g["ln_a_g"][0]), by_partition(g["ln_a_b"][0]),
        by_partition(g["conv_b_w"][0]).transpose(0, 2, 1).reshape(P, KA * TAPS_B),
        by_partition(g["pool_b"][0]), by_partition(g["pool_scale"][0]),
    ], axis=1)

    def history(v):
        return by_partition(v).transpose(0, 3, 1, 2)

    data = {
        "x_t": by_partition(tokens).transpose(0, 2, 1), "par": par,
        "hist_a": history(g["state_conv_a"][0]), "hist_b": history(g["state_conv_b"][0]),
        "hist_c": history(g["state_pool"][0]),
        "ffn_w_in": g["ffn_w_in"], "ffn_w_out": g["ffn_w_out"], "mix_w_in": g["mix_w_in"],
        "mix_w_out": g["mix_w_out"], "pool_w": g["pool_w"],
    }
    data = {k: np.ascontiguousarray(v) for k, v in data.items()}

    nc = bacc.Bacc("TRN2", target_bir_lowering=False, num_devices=1)
    aps = {k: nc.dram_tensor(k, s, F32, kind="ExternalInput").ap() for k, s in INPUTS.items()}
    aps |= {k: nc.dram_tensor(k, s, F32, kind="ExternalOutput").ap() for k, s in OUTPUTS.items()}
    build(nc, aps)
    got = run_bass_kernel_spmd(nc, [data], core_ids=[0]).results[0]

    y = got["y_t"].transpose(2, 1, 0).reshape(T, D)

    def prompt_rows(v):
        return np.ascontiguousarray(v.transpose(2, 1, 0).reshape(1, 1, v.shape[2], -1))

    def sample_rows(v):
        return np.ascontiguousarray(v.transpose(2, 3, 1, 0).reshape(1, SEQS, v.shape[3], -1))

    return (np.ascontiguousarray(y[:PROMPT].reshape(1, PROMPT, D)),
            np.ascontiguousarray(y[PROMPT:].reshape(SEQS, STEP, D)),
            prompt_rows(got["new_a_prompt"]), prompt_rows(got["new_b_prompt"]), prompt_rows(got["new_c_prompt"]),
            sample_rows(got["new_a_sample"]), sample_rows(got["new_b_sample"]), sample_rows(got["new_c_sample"]))
```

```python
from contextlib import ExitStack

import concourse.bass as bass
from concourse import mybir

F32 = mybir.dt.float32
F32R = mybir.dt.float32r
ALU = mybir.AluOpType
ACT = mybir.ActivationFunctionType

P = 128
PROMPT, SEQS, STEP = 256, 8, 4
T = PROMPT + SEQS * STEP
D = 1024
KD = D // P
DFF = 2816
KF = DFF // P
DA = 512
KA = DA // P
TAPS_A, TAPS_B = 31, 3
HA, HB, HC = TAPS_A - 1, TAPS_B - 1, 15
WINDOWS = (2, 4, 8, 16)
EPS = 1e-6

RING, SLOT = 4, 2048
UNITS = KF // 2
IN_CHUNKS = 2 * UNITS
QUARTERS = 4
Q_SPLIT = ((0, 6), (6, 12), (12, 18), (18, 22))
OUT_CHUNKS = QUARTERS * len(Q_SPLIT)
FFN_CHUNKS = IN_CHUNKS + OUT_CHUNKS
A_UNITS = 10
A_CHUNKS = A_UNITS + 4
FFN_BASE = (0, FFN_CHUNKS + A_CHUNKS, 2 * FFN_CHUNKS + A_CHUNKS, 3 * FFN_CHUNKS + A_CHUNKS + 1)
A_BASE = FFN_CHUNKS
C_BASE = 3 * FFN_CHUNKS + A_CHUNKS
CHUNKS = C_BASE + 1 + FFN_CHUNKS

SPLIT_NORMS = (0, 1, 2, 3, 5)
DIRECT_NORMS = (0, 5)
FFN_NORM = (0, 2, 3, 5)
NEXT_NORM = (1, 3, 4, 6)

SUM_STEPS = KD - 1

STAT_BANK, R_BANK = 4, 2
A_OUT_BANK = (3, 0, 1, 2, 4, 5, 6, 7)
LN_BANK = (4, 5, 7, 4)

PC_G, PC_WA, PC_BA, PC_LG, PC_LB, PC_WB, PC_PB, PC_PS = 0, 56, 180, 184, 188, 192, 204, 212
PARAMS = 220


def sum_bank(n):
    return 3 if n > 0 else 5


def out_bank(m):
    return 4 + m % 4


def build(nc, a):
    ctx = ExitStack()
    with ctx:
        def sb(name, shape, dt=F32):
            return ctx.enter_context(nc.sbuf_tensor(name, shape, dt))

        def sem(name):
            return ctx.enter_context(nc.semaphore(name))

        w_raw = sb("w_raw", [P, RING, SLOT])
        w_hi = sb("w_hi", [P, RING, SLOT], F32R)
        w_lo = sb("w_lo", [P, RING, SLOT], F32R)
        x = sb("x", [P, KD, T])
        x_hi = sb("x_hi", [P, KD, T], F32R)
        x_lo = sb("x_lo", [P, KD, T], F32R)
        h_hi = sb("h_hi", [P, KF, T], F32R)
        h_lo = sb("h_lo", [P, KF, T], F32R)
        scaled = sb("scaled", [P, 2, T])
        acted = sb("acted", [P, 2, T])
        norm_buf = sb("norm_buf", [P, 4, T])
        squares, rms, square_sum = norm_buf[:, 0:2, :], norm_buf[:, 2, :], norm_buf[:, 3, :]
        r = sb("r", [P, T])
        ones = sb("ones", [P, P])
        ident = sb("ident", [P, P])
        taps_hi = sb("taps_hi", [P, TAPS_A], F32R)
        taps_lo = sb("taps_lo", [P, TAPS_A])
        eps = sb("eps", [P, 1])
        primed = sb("primed", [P, 1])
        par = sb("par_sb", [P, PARAMS])
        bias_scaled = sb("bias_scaled", [P, KD])
        count_i = sb("count_i", [P, HC], mybir.dt.int32)
        inv_count = sb("inv_count", [P, len(WINDOWS), HC])
        head = sb("head", [P, 2, HC])
        mix = sb("mix", [P, 5760])
        psum = ctx.enter_context(nc.psum_tensor("psum", [P, 8, 512], F32))

        ea_w, eb_w = HA + PROMPT + SEQS * (HA + STEP), HB + PROMPT + SEQS * (HB + STEP)
        ext_a = mix[:, 0:KA * ea_w].rearrange("p (i n) -> p i n", i=KA)
        eb0 = KA * ea_w
        ext_b = mix[:, eb0:eb0 + KA * eb_w].rearrange("p (i n) -> p i n", i=KA)
        y0 = eb0 + KA * eb_w
        y_a = mix[:, y0:y0 + KA * T].rearrange("p (i n) -> p i n", i=KA)
        y_b = mix[:, y0 + KA * T:y0 + 2 * KA * T].rearrange("p (i n) -> p i n", i=KA)
        ln_sq = y_b
        row_hi, row_lo = (h[:, 0:2, :].rearrange("p a b -> p (a b)")[:, 0:HA + PROMPT] for h in (h_hi, h_lo))
        diag_hi, diag_lo = (
            h[:, KD:KF, :].rearrange("p a b -> p (a b)")[:, 0:TAPS_A * P].rearrange("p (k n) -> p k n", k=TAPS_A)
            for h in (h_hi, h_lo))
        n_prod = SEQS * STEP * TAPS_A
        tap_prod = norm_buf[:, :, :].rearrange("p a b -> p (a b)")[:, 0:n_prod].rearrange(
            "p (s t k) -> p s t k", s=SEQS, t=STEP)
        ec_w = HC + PROMPT + SEQS * (HC + STEP)
        ext_c = mix[:, 0:KD * ec_w].rearrange("p (i n) -> p i n", i=KD)
        win = [mix[:, (KD + 2 * z) * ec_w:(KD + 2 * z + 2) * ec_w].rearrange("p (i n) -> p i n", i=2)
               for z in range(2)]
        y_out = mix[:, 0:KD * T].rearrange("p (i n) -> p i n", i=KD)

        def prompt_of(ext, i, hist, at, n=PROMPT):
            return ext[:, i, at:at + n]

        def sample_of(ext, i, hist, at, n=STEP):
            s = ext[:, i, hist + PROMPT:hist + PROMPT + SEQS * (hist + STEP)]
            return s.rearrange("p (s n) -> p s n", s=SEQS)[:, :, at:at + n]

        def bank(b, lo=0, hi=T):
            return psum[:, b, lo:hi]

        def sample_cols(ap):
            return ap.rearrange("p (s n) -> p s n", s=SEQS)

        def pcol(c):
            return par[:, c:c + 1]

        w_landed = [sem(f"w_landed{i}") for i in range(RING)]
        w_high = sem("w_high")
        w_low = sem("w_low")
        w_used = sem("w_used")
        w_first = sem("w_first")
        first_high = sem("first_high")
        first_low = sem("first_low")
        x_landed = [sem(f"x_landed{i}") for i in range(2)]
        par_landed = sem("par_landed")
        hist_ab_landed = sem("hist_ab_landed")
        hist_c_landed = sem("hist_c_landed")
        consts_set = sem("consts_set")
        pads_set = sem("pads_set")
        count_set = sem("count_set")
        x_new = sem("x_new")
        xg_ready = sem("xg_ready")
        x_high = sem("x_high")
        x_low = sem("x_low")
        squared = sem("squared")
        sum_step = sem("sum_step")
        stat_full = sem("stat_full")
        rms_ready = sem("rms_ready")
        r_ready = sem("r_ready")
        pair_full = sem("pair_full")
        gate_scaled = sem("gate_scaled")
        up_scaled = sem("up_scaled")
        gate_acted = sem("gate_acted")
        hid_ready = sem("hid_ready")
        hid_high = sem("hid_high")
        hid_low = sem("hid_low")
        a_gate_scaled = sem("a_gate_scaled")
        a_gate_acted = sem("a_gate_acted")
        a_evacuated = sem("a_evacuated")
        conv_prompt = sem("conv_prompt")
        tap_products = sem("tap_products")
        taps_high = sem("taps_high")
        taps_low = sem("taps_low")
        diag_ready = sem("diag_ready")
        row_high = sem("row_high")
        row_low = sem("row_low")
        conv_pe_full = sem("conv_pe_full")
        conv_pe_ready = sem("conv_pe_ready")
        ident_zero = sem("ident_zero")
        ident_set = sem("ident_set")
        conv_sample_sum = sem("conv_sample_sum")
        conv_sample = sem("conv_sample")
        x_biased = sem("x_biased")
        prime_done = sem("prime_done")
        y_ready = sem("y_ready")
        y_high = sem("y_high")
        y_low = sem("y_low")
        ln_sum_full = sem("ln_sum_full")
        ln_centred = sem("ln_centred")
        ln_squared = sem("ln_squared")
        ln_var_full = sem("ln_var_full")
        ln_std_ready = sem("ln_std_ready")
        ln_scaled = sem("ln_scaled")
        a_out_full = sem("a_out_full")
        a_state_out = sem("a_state_out")
        c_h_ready = sem("c_h_ready")
        pooled_ready = sem("pooled_ready")
        pooled_high = sem("pooled_high")
        pooled_low = sem("pooled_low")
        c_out_full = sem("c_out_full")
        c_state_out = sem("c_state_out")
        y_done = sem("y_done")
        out_stored = sem("out_stored")
        own = sem("own")

        block = ctx.enter_context(nc.Block())

        def x_low_count(n, tiles):
            return KD * SPLIT_NORMS.index(n) + tiles

        def x_new_count(n, tiles):
            return KD * (n - 1) + tiles

        @block.sync
        def _(sp):
            def slot_free(c, more=0):
                sp.wait_ge(w_low, c - RING + 1 + more)

            def load(c, dst0, src0, dst1, src1):
                sp.dma_start(dst0, src0).then_inc(w_landed[c % RING], 16)
                sp.dma_start(dst1, src1).then_inc(w_landed[c % RING], 16)

            def load_in(f, c, half, unit):
                w = a["ffn_w_in"][f // 2, f % 2].rearrange("(k p) (g n) -> p k g n", p=P, g=2)
                dst = w_raw[:, c % RING, :].rearrange("p (k g n) -> p k g n", k=4, g=2)
                k = slice(4 * half, 4 * half + 4)
                cols = bass.ds(unit * 2 * P, 2 * P)
                load(c, dst[:, :, 0, :], w[:, k, 0, cols], dst[:, :, 1, :], w[:, k, 1, cols])

            def first_loads():
                w = a["ffn_w_in"][0, 0].rearrange("(k p) (g n) -> p k g n", p=P, g=2)
                dst = w_raw[:, 0, :].rearrange("p (k g n) -> p k g n", k=4, g=2)
                for half, landed in ((0, w_first), (1, w_landed[0])):
                    k = slice(2 * half, 2 * half + 2)
                    for g in range(2):
                        sp.dma_start(dst[:, k, g, :], w[:, k, g, 0:2 * P]).then_inc(landed, 16)
                    tiles = slice(4 * half, 4 * half + 4)
                    sp.dma_start(x[:, tiles, :], a["x_t"][:, tiles, :]).then_inc(x_landed[half], 16)

            def load_out(f, c, part, quarter):
                w = a["ffn_w_out"][f // 2, f % 2].rearrange("(k p) n -> p k n", p=P)
                k0, k1 = Q_SPLIT[part]
                km = (k0 + k1) // 2
                dst = w_raw[:, c % RING, 0:(k1 - k0) * 2 * P].rearrange("p (k n) -> p k n", n=2 * P)
                cols = bass.ds(quarter * 2 * P, 2 * P)
                load(c, dst[:, 0:km - k0, :], w[:, k0:km, cols], dst[:, km - k0:k1 - k0, :], w[:, km:k1, cols])

            def ffn(f, small):
                base = FFN_BASE[f]
                if f == 0:
                    first_loads()
                for j in range(1 if f == 0 else 0, RING):
                    if f > 0:
                        slot_free(base + j)
                    load_in(f, base + j, j % 2, j // 2)
                small()
                with sp.Fori(0, UNITS // 2 - 1) as i:
                    for j in range(RING, 2 * RING):
                        slot_free(base + j, 4 * i)
                        load_in(f, base + j, j % 2, 2 * i + j // 2)
                for j in range(4 * (UNITS // 2), IN_CHUNKS):
                    slot_free(base + j)
                    load_in(f, base + j, j % 2, j // 2)
                base += IN_CHUNKS
                with sp.Fori(0, QUARTERS) as q:
                    for j in range(RING):
                        slot_free(base + j, 4 * q)
                        load_out(f, base + j, j, q)

            def mixer_a():
                w = a["mix_w_in"][0].rearrange("(k p) n -> p k n", p=P)
                for v in range(A_UNITS):
                    c = A_BASE + v
                    slot_free(c)
                    dst = w_raw[:, c % RING, :].rearrange("p (k g n) -> p k g n", k=KD, g=2)
                    if v < 2 * KA:
                        c0 = (0 if v < KA else 3 * DA) + v % KA * P
                        load(c, dst[:, :, 0, :], w[:, :, c0:c0 + P], dst[:, :, 1, :], w[:, :, c0 + DA:c0 + DA + P])
                    else:
                        c0 = 2 * DA + (v - 2 * KA) * 2 * P
                        dst = w_raw[:, c % RING, :].rearrange("p (k n) -> p k n", k=KD)
                        load(c, dst[:, 0:4, :], w[:, 0:4, c0:c0 + 2 * P], dst[:, 4:8, :], w[:, 4:8, c0:c0 + 2 * P])
                w = a["mix_w_out"][0].rearrange("(k p) n -> p k n", p=P)
                for o in range(4):
                    c = A_BASE + A_UNITS + o
                    slot_free(c)
                    k0, c0 = (KA, 0)[o % 2], o // 2 * 512
                    dst = w_raw[:, c % RING, :].rearrange("p (k n) -> p k n", k=KA)
                    load(c, dst[:, 0:2, :], w[:, k0:k0 + 2, c0:c0 + 512],
                         dst[:, 2:4, :], w[:, k0 + 2:k0 + 4, c0:c0 + 512])

            def mixer_c():
                slot_free(C_BASE)
                w = a["pool_w"][0].rearrange("g (k p) n -> p (g k) n", p=P)
                dst = w_raw[:, C_BASE % RING, :].rearrange("p (k n) -> p k n", k=KD)
                load(C_BASE, dst[:, 0:4, :], w[:, 0:4, :], dst[:, 4:8, :], w[:, 4:8, :])

            def history_ab():
                for i in range(KA):
                    sp.dma_start(sample_of(ext_a, i, HA, 0, HA), a["hist_a"][:, i, :, :]).then_inc(hist_ab_landed, 16)
                    sp.dma_start(sample_of(ext_b, i, HB, 0, HB), a["hist_b"][:, i, :, :]).then_inc(hist_ab_landed, 16)

            def mixer_a_state():
                sp.wait_ge(a_evacuated, 2 * KA)
                sp.wait_ge(hist_ab_landed, 16 * 2 * KA)
                for i in range(KA):
                    sp.dma_start(a["new_a_prompt"][:, i, :], ext_a[:, i, PROMPT:PROMPT + HA]).then_inc(a_state_out, 16)
                    sp.dma_start(a["new_a_sample"][:, i, :, :], sample_of(ext_a, i, HA, STEP, HA)).then_inc(a_state_out, 16)
                    sp.dma_start(a["new_b_prompt"][:, i, :], ext_b[:, i, PROMPT:PROMPT + HB]).then_inc(a_state_out, 16)
                    sp.dma_start(a["new_b_sample"][:, i, :, :], sample_of(ext_b, i, HB, STEP, HB)).then_inc(a_state_out, 16)

            def history_c():
                sp.wait_ge(a_state_out, 16 * 4 * KA)
                sp.wait_ge(y_low, KD)
                for m in range(KD):
                    sp.dma_start(sample_of(ext_c, m, HC, 0, HC), a["hist_c"][:, m, :, :]).then_inc(hist_c_landed, 16)

            def mixer_c_state():
                sp.wait_ge(c_h_ready, KD)
                for m in range(KD):
                    sp.dma_start(a["new_c_prompt"][:, m, :], ext_c[:, m, PROMPT:PROMPT + HC]).then_inc(c_state_out, 16)
                    sp.dma_start(a["new_c_sample"][:, m, :, :], sample_of(ext_c, m, HC, STEP, HC)).then_inc(c_state_out, 16)

            ffn(0, history_ab)
            mixer_a()
            ffn(1, mixer_a_state)
            ffn(2, history_c)
            mixer_c()
            ffn(3, mixer_c_state)
            sp.wait_ge(c_state_out, 16 * 2 * KD)
            for m in range(0, KD, 2):
                sp.wait_ge(y_done, m + 2)
                sp.dma_start(a["y_t"][:, m:m + 2, :], y_out[:, m:m + 2, :]).then_inc(out_stored, 16)
            sp.wait_ge(out_stored, 16 * KD // 2)

        @block.gpsimd
        def _(pool):
            pool.memset(ones[:, :], 1.0)
            pool.memset(eps[:, :], EPS).then_inc(consts_set, 1)
            pool.memset(ext_a[:, :, 0:HA], 0.0)
            pool.memset(ext_b[:, :, 0:HB], 0.0).then_inc(pads_set, 1)
            pool.iota(count_i[:, :], pattern=[[1, HC]], base=1, channel_multiplier=0).then_inc(count_set, 1)

            def low(c, n, more=0):
                pool.wait_ge(w_high, c + 1 + more)
                s = c % RING
                pool.tensor_tensor(w_lo[:, s, 0:n], w_raw[:, s, 0:n], w_hi[:, s, 0:n].bitcast(F32),
                                   ALU.subtract).then_inc(w_low, 1)

            pool.memset(ident[:, :], 0.0).then_inc(ident_zero, 1)
            pool.wait_ge(ident_zero, 1)
            pool.affine_select(out=ident[:, :], in_=ident[:, :], compare_op=ALU.not_equal, fill=1.0, base=0,
                               pattern=[[-1, P]], channel_multiplier=1).then_inc(ident_set, 1)

            def first():
                for k in range(4):
                    if k < 3:
                        pool.wait_ge(first_high, k + 1)
                    else:
                        pool.wait_ge(w_high, 1)
                    cols = slice(k * 4 * P, (k + 1) * 4 * P)
                    pool.tensor_tensor(w_lo[:, 0, cols], w_raw[:, 0, cols], w_hi[:, 0, cols].bitcast(F32),
                                       ALU.subtract).then_inc(first_low if k < 3 else w_low, 1)

            def ffn(f):
                base = FFN_BASE[f]
                if f == 0:
                    first()
                for j in range(1 if f == 0 else 0, RING):
                    low(base + j, SLOT)
                with pool.Fori(0, UNITS // 2 - 1) as i:
                    for j in range(RING, 2 * RING):
                        low(base + j, SLOT, 4 * i)
                for j in range(4 * (UNITS // 2), IN_CHUNKS):
                    low(base + j, SLOT)
                base += IN_CHUNKS
                with pool.Fori(0, QUARTERS) as q:
                    for j in range(RING):
                        low(base + j, (Q_SPLIT[j][1] - Q_SPLIT[j][0]) * 2 * P, 4 * q)

            def tap_product(i):
                pool.wait_ge(a_evacuated, i + 1)
                if i == 0:
                    pool.wait_ge(par_landed, 16)
                    pool.wait_ge(hist_ab_landed, 16 * 2 * KA)
                else:
                    pool.wait_ge(conv_sample_sum, i)
                row = sample_of(ext_a, i, HA, 0)
                under = bass.AP(row.tensor, row.offset, [[5760, P], [HA + STEP, SEQS], [1, STEP], [1, TAPS_A]])
                taps = par[:, PC_WA + TAPS_A * i:PC_WA + TAPS_A * (i + 1)]
                taps = taps.unsqueeze(1).unsqueeze(1).broadcast_to([P, SEQS, STEP, TAPS_A])
                pool.tensor_tensor(tap_prod, under, taps, ALU.mult).then_inc(tap_products, 1)

            ffn(0)
            for c in range(A_BASE, A_BASE + A_CHUNKS):
                low(c, SLOT)
                if c == A_BASE:
                    pool.wait_ge(taps_high, 1)
                    pool.tensor_tensor(taps_lo[:, :], par[:, PE_COLS:PE_COLS + TAPS_A], taps_hi[:, :].bitcast(F32),
                                       ALU.subtract).then_inc(taps_low, 1)
                if c - A_BASE == ROW_AT:
                    pool.wait_ge(row_high, 1)
                    pool.tensor_tensor(row_lo, ext_a[:, PE_TILE, 0:HA + PROMPT], row_hi.bitcast(F32),
                                       ALU.subtract).then_inc(row_low, 1)
                if c - A_BASE in PRODUCTS_AT:
                    tap_product(PRODUCTS_AT.index(c - A_BASE))
            ffn(1)
            ffn(2)
            low(C_BASE, SLOT)
            ffn(3)

        def chunk_cols(c):
            for base in FFN_BASE:
                if base + IN_CHUNKS <= c < base + FFN_CHUNKS:
                    k0, k1 = Q_SPLIT[(c - base - IN_CHUNKS) % 4]
                    return (k1 - k0) * 2 * P
            return SLOT

        @block.scalar
        def _(act):
            def high(c, i=None):
                if c >= CHUNKS:
                    return
                more = 0 if i is None else i
                n = chunk_cols(c)
                act.wait_ge(w_landed[c % RING], 32 * (c // RING + 1) + 32 * more)
                if c >= RING:
                    act.wait_ge(w_used, c - RING + 1 + RING * more)
                act.activation(w_hi[:, c % RING, 0:n], w_raw[:, c % RING, 0:n], ACT.Copy).then_inc(w_high, 1)

            def norm_tile(n, m):
                if n == 0:
                    act.wait_ge(x_landed[m // 4], 16)
                else:
                    act.wait_ge(x_new, x_new_count(n, m + 1))
                if n in DIRECT_NORMS:
                    act.activation(x_hi[:, m, :], x[:, m, :], ACT.Copy,
                                   scale=pcol(PC_G + KD * n + m)).then_inc(x_high, 1)
                elif n in SPLIT_NORMS:
                    act.wait_ge(xg_ready, KD * (n - 1) + m + 1)
                    b = A_OUT_BANK[m] if n == 2 else out_bank(m)
                    act.activation(x_hi[:, m, :], bank(b), ACT.Copy).then_inc(x_high, 1)
                if m == 0 and n == 2:
                    act.wait_ge(x_low, x_low_count(n, 1))
                if m >= 3:
                    act.wait_ge(sum_step, SUM_STEPS * n + m - 2)
                dst = bank(sum_bank(n)) if m == 0 else squares[:, m % 2, :]
                act.activation(dst, x[:, m, :], ACT.Square).then_inc(squared, 1)

            primes = [0]

            def prime(func):
                if primes[0]:
                    act.wait_ge(prime_done, primes[0])
                primes[0] += 1
                act.activation(primed[:, :], eps[:, :], func).then_inc(prime_done, 1)

            def root(n):
                act.wait_ge(stat_full, n + 1)
                act.activation(rms, bank(STAT_BANK), ACT.Sqrt, bias=eps[:, :],
                               scale=1.0 / D).then_inc(rms_ready, 1)

            def hidden(f, b, z, j, pairs_before):
                act.wait_ge(gate_scaled, pairs_before + 1)
                act.activation(acted[:, z, :], scaled[:, z, :], ACT.Silu).then_inc(gate_acted, 1)
                act.wait_ge(hid_ready, pairs_before + 1)
                act.activation(h_hi[:, j, :], bank(b), ACT.Copy).then_inc(hid_high, 1)

            def hidden_at(f, p, i=None):
                b = 4 * (p // 2 % 2) + 2 * (p % 2)
                if i is None:
                    hidden(f, b, p % 2, p, KF * f + p)
                else:
                    hidden(f, b, p % 2, bass.ds(4 * i + p, 1), 4 * i + (KF * f + p))

            def ffn(f):
                base = FFN_BASE[f]
                root(FFN_NORM[f])
                prime(ACT.Silu)
                high(base + RING)
                high(base + RING + 1)
                hidden_at(f, 0)
                hidden_at(f, 1)
                for p in range(2, 4):
                    high(base + RING + p)
                    hidden_at(f, p)
                with act.Fori(0, 3) as i:
                    for p in range(4, 8):
                        high(base + RING + p, i)
                        hidden_at(f, p, i)
                for p in range(16, IN_CHUNKS):
                    high(base + RING + p)
                    hidden_at(f, p)
                base += IN_CHUNKS
                prime(ACT.Sqrt)
                for q in range(QUARTERS):
                    for j in range(3):
                        high(base + 4 * q + j + RING)
                    for m in (2 * q, 2 * q + 1):
                        norm_tile(NEXT_NORM[f], m)
                    if q == QUARTERS - 1 and NEXT_NORM[f] not in SPLIT_NORMS:
                        root(NEXT_NORM[f])
                    high(base + 4 * q + 3 + RING)

            def split_y(k, b):
                act.activation(h_hi[:, k, :], bank(b), ACT.Copy).then_inc(y_high, 1)

            def mixer_a():
                root(1)
                prime(ACT.Sigmoid)
                high(A_BASE + RING)
                for v in range(A_UNITS):
                    if v > 0:
                        high(A_BASE + RING + v)
                    if v < KA:
                        act.wait_ge(a_gate_scaled, v + 1)
                        act.activation(acted[:, v % 2, :], scaled[:, v % 2, :], ACT.Sigmoid).then_inc(a_gate_acted, 1)
                    elif v >= 2 * KA:
                        for t in range(2):
                            i = 2 * (v - 2 * KA) + t
                            act.wait_ge(y_ready, i + 1)
                            split_y(KA + i, 2 * (v % 2) + t)
                    if v == KA:
                        act.wait_ge(a_evacuated, KA)
                        act.wait_ge(hist_ab_landed, 16 * 2 * KA)
                        act.wait_ge(pads_set, 1)
                        act.activation(row_hi, ext_a[:, PE_TILE, 0:HA + PROMPT], ACT.Copy).then_inc(row_high, 1)
                    if v == 0:
                        act.wait_ge(taps_low, 1)
                        act.wait_ge(taps_high, 1)
                        act.wait_ge(ident_set, 1)
                    for k in range(DIAGS_AT_ONCE * v, min(DIAGS_AT_ONCE * (v + 1), TAPS_A)):
                        act.activation(diag_hi[:, k, :], ident[:, :], ACT.Copy, scale=taps_hi[:, k:k + 1].bitcast(F32))
                        act.activation(diag_lo[:, k, :], ident[:, :], ACT.Copy,
                                       scale=taps_lo[:, k:k + 1]).then_inc(diag_ready, 1)
                act.wait_ge(conv_pe_full, 1)
                act.activation(y_a[:, PE_TILE, 0:PROMPT], bank(4 + PE_TILE, 0, PROMPT), ACT.Identity,
                               bias=pcol(PC_BA + PE_TILE)).then_inc(conv_pe_ready, 1)
                prime(ACT.Sqrt)
                for i in range(KA):
                    act.wait_ge(ln_centred, i + 1)
                    act.activation(ln_sq[:, i, :], y_a[:, i, :], ACT.Square).then_inc(ln_squared, 1)
                act.wait_ge(ln_var_full, 1)
                act.activation(rms, bank(5), ACT.Sqrt, bias=eps[:, :], scale=1.0 / DA).then_inc(ln_std_ready, 1)
                prime(ACT.Silu)
                for i in range(KA):
                    act.wait_ge(ln_scaled, i + 1)
                    if i == 3:
                        act.wait_ge(y_low, KA + 1)
                    act.activation(bank(LN_BANK[i]), y_a[:, i, :], ACT.Silu, bias=pcol(PC_LB + i),
                                   scale=pcol(PC_LG + i)).then_inc(y_ready, 1)
                    act.wait_ge(y_ready, KA + i + 1)
                    split_y(i, LN_BANK[i])
                prime(ACT.Sqrt)
                high(A_BASE + A_UNITS + RING)
                high(A_BASE + A_UNITS + 1 + RING)
                for m in range(KA):
                    norm_tile(2, m)
                high(A_BASE + A_UNITS + 2 + RING)
                for m in range(KA, KD - 1):
                    norm_tile(2, m)
                norm_tile(2, KD - 1)
                high(A_BASE + A_UNITS + 3 + RING)

            def mixer_c():
                for g in range(4):
                    tiles = (2 * g, 2 * g + 1)
                    for m in tiles:
                        act.wait_ge(c_h_ready, m + 1)
                        act.activation(x[:, m, :], x[:, m, :], ACT.Identity,
                                       bias=bias_scaled[:, m:m + 1]).then_inc(x_biased, 1)
                    if g > 1:
                        norm_tile(5, 2 * g - 4)
                        norm_tile(5, 2 * g - 3)
                    for m in tiles:
                        act.wait_ge(pooled_ready, m + 1)
                        act.activation(h_hi[:, m, :], bank(m % 2), ACT.Copy).then_inc(pooled_high, 1)
                for m in range(KD - 4, KD):
                    norm_tile(5, m)
                high(C_BASE + RING)

            act.dma_start(par[:, :], a["par"]).then_inc(par_landed, 16)
            act.wait_ge(consts_set, 1)
            prime(ACT.Sqrt)

            def first(k):
                act.wait_ge(w_first if k < 2 else w_landed[0], 32)
                cols = slice(k * 4 * P, (k + 1) * 4 * P)
                act.activation(w_hi[:, 0, cols], w_raw[:, 0, cols], ACT.Copy).then_inc(first_high if k < 3 else w_high, 1)

            first(0)
            first(1)
            act.wait_ge(par_landed, 16)
            for m in range(4):
                norm_tile(0, m)
                if m % 2 == 1:
                    first(2 + m // 2)
            high(1)
            for m in range(4, KD):
                norm_tile(0, m)
            high(2)
            high(3)
            act.activation(taps_hi[:, :], par[:, PE_COLS:PE_COLS + TAPS_A], ACT.Copy).then_inc(taps_high, 1)
            ffn(0)
            mixer_a()
            ffn(1)
            ffn(2)
            mixer_c()
            ffn(3)

        @block.tensor
        def _(pe):
            def product(b, s, col, hi, lo, k, first, last):
                w_h, w_l = w_hi[:, s, col:col + P], w_lo[:, s, col:col + P]
                pe.matmul(bank(b), w_h, hi[:, k, :], start=first, stop=False)
                pe.matmul(bank(b), w_h, lo[:, k, :], start=False, stop=False)
                return pe.matmul(bank(b), w_l, hi[:, k, :], start=False, stop=last)

            def stat(n):
                pe.wait_ge(sum_step, SUM_STEPS * (n + 1))
                pe.matmul(bank(STAT_BANK), ones[:, :], square_sum, start=True, stop=True).then_inc(stat_full, 1)

            def unit_half(c, banks, half, more=0, before_last=None):
                pe.wait_ge(w_low, c + 1 + more)
                for z in range(4):
                    g, pair = z % 2, z // 2
                    if z == 3 and before_last is not None:
                        before_last()
                    for k in range(4):
                        mm = product(banks + z, c % RING, (2 * k + g) * 2 * P + pair * P, x_hi, x_lo, 4 * half + k,
                                     half == 0 and k == 0, half == 1 and k == 3)
                    if half == 1 and z == 1:
                        mm.then_inc(pair_full, 1)
                mm.then_inc(w_used, 1)

            def ffn(f):
                base, n = FFN_BASE[f], FFN_NORM[f]
                if f == 0:
                    for k in range(4):
                        pe.wait_ge(first_low if k < 3 else w_low, k + 1 if k < 3 else 1)
                        pe.wait_ge(x_low, k + 1)
                        for z in range(4):
                            mm = product(z, 0, (2 * k + z % 2) * 2 * P + z // 2 * P, x_hi, x_lo, k, k == 0, False)
                    mm.then_inc(w_used, 1)
                else:
                    pe.wait_ge(x_low, x_low_count(n, 4))
                    unit_half(base, 0, 0, before_last=lambda: pe.wait_ge(sum_step, SUM_STEPS * (n + 1)))
                pe.wait_ge(x_low, x_low_count(n, KD))
                stat(n)
                unit_half(base + 1, 0, 1)
                pe.wait_ge(r_ready, n + 1)
                unit_half(base + 2, 4, 0)
                unit_half(base + 3, 4, 1)
                with pe.Fori(0, UNITS // 2 - 1) as i:
                    for j in range(4, 8):
                        if j % 2 == 0:
                            pe.wait_ge(hid_low, 4 * i + (KF * f + j - 2))
                        unit_half(base + j, 4 * (j // 2 % 2), j % 2, 4 * i)
                pe.wait_ge(hid_low, KF * f + 2 * (UNITS - 2))
                unit_half(base + IN_CHUNKS - 2, 0, 0)
                unit_half(base + IN_CHUNKS - 1, 0, 1)
                base += IN_CHUNKS
                pe.wait_ge(hid_low, KF * f + 2 * (UNITS - 1))
                nn = NEXT_NORM[f]
                with pe.Fori(0, QUARTERS // 2) as i:
                    for q in range(2):
                        if nn in SPLIT_NORMS:
                            pe.wait_ge(x_low, 4 * i + x_low_count(nn, 2 * q - 2))
                        else:
                            pe.wait_ge(x_new, 4 * i + x_new_count(nn, 2 * q - 2))
                        for part, (k0, k1) in enumerate(Q_SPLIT):
                            c = base + 4 * q + part
                            pe.wait_ge(w_low, 8 * i + c + 1)
                            if q == 0 and part == 3:
                                pe.wait_ge(hid_low, KF * (f + 1))
                            for z in range(2):
                                for k in range(k0, k1):
                                    mm = product(4 + 2 * q + z, c % RING, (k - k0) * 2 * P + z * P, h_hi, h_lo, k,
                                                 k == 0, k == KF - 1)
                            mm.then_inc(w_used, 1)

            def mixer_a():
                for v in range(A_UNITS):
                    c = A_BASE + v
                    banks = 2 * (v % 2)
                    if v == 1:
                        stat(1)
                    if v >= 2:
                        pe.wait_ge(a_evacuated, v - 1)
                    pe.wait_ge(w_low, c + 1)
                    for k in range(KD):
                        if v == 0:
                            pe.wait_ge(x_low, x_low_count(1, k + 1))
                        for z in range(2):
                            mm = product(banks + z, c % RING, (2 * k + z) * P, x_hi, x_lo, k, k == 0, k == KD - 1)
                    mm.then_inc(w_used, 1)
                base = A_BASE + A_UNITS

                def late_part(c):
                    for k in range(KA):
                        pe.wait_ge(y_low, KA + k + 1)
                        for m in range(KA):
                            mm = product(A_OUT_BANK[m], c % RING, k * 512 + m * P, h_hi, h_lo, k, False, k == KA - 1)
                            if k == KA - 1:
                                mm.then_inc(a_out_full if m < KA - 1 else w_used, 1)

                def part(c, tiles, k_base, first, whole=True):
                    for m in tiles:
                        for k in range(KA):
                            mm = product(A_OUT_BANK[m], c % RING, k * 512 + m % 4 * P, h_hi, h_lo, k_base + k,
                                         first and k == 0, not first and k == KA - 1)
                        if not first and m % 4 < 3:
                            mm.then_inc(a_out_full, 1)
                    if whole:
                        mm.then_inc(w_used, 1)

                pe.wait_ge(diag_ready, TAPS_A)
                pe.wait_ge(row_low, 1)
                b = 4 + PE_TILE
                for k in range(TAPS_A):
                    out = bank(b, 0, PROMPT)
                    pe.matmul(out, diag_hi[:, k, :], row_hi[:, k:k + PROMPT], start=k == 0, stop=False)
                    pe.matmul(out, diag_hi[:, k, :], row_lo[:, k:k + PROMPT], start=False, stop=False)
                    mm = pe.matmul(out, diag_lo[:, k, :], row_hi[:, k:k + PROMPT], start=False, stop=k == TAPS_A - 1)
                mm.then_inc(conv_pe_full, 1)
                for i in range(KA):
                    if i == PE_TILE:
                        pe.wait_ge(conv_pe_ready, 1)
                    else:
                        pe.wait_ge(conv_prompt, CONV_STEPS * (i + 1))
                    pe.wait_ge(conv_sample, i + 1)
                    mm = pe.matmul(bank(4), ones[:, :], y_a[:, i, :], start=i == 0, stop=i == KA - 1)
                mm.then_inc(ln_sum_full, 1)
                pe.wait_ge(y_low, KA)
                pe.wait_ge(w_low, base + 1)
                part(base, (0, 1), KA, True, whole=False)
                for i in range(KA):
                    pe.wait_ge(ln_squared, i + 1)
                    mm = pe.matmul(bank(5), ones[:, :], ln_sq[:, i, :], start=i == 0, stop=i == KA - 1)
                mm.then_inc(ln_var_full, 1)
                part(base, (2, 3), KA, True)
                pe.wait_ge(w_low, base + 2)
                late_part(base + 1)
                pe.wait_ge(w_low, base + 3)
                part(base + 2, range(KA, KD), KA, True)
                pe.wait_ge(w_low, base + 4)
                part(base + 3, range(KA, KD), 0, False)

            def mixer_c():
                stat(4)
                pe.wait_ge(w_low, C_BASE + 1)
                for g in range(4):
                    pe.wait_ge(pooled_low, 2 * g + 2)
                    if g >= 2:
                        pe.wait_ge(x_low, x_low_count(5, 2 * g - 2))
                    for z in range(2):
                        for k in range(2):
                            mm = product(out_bank(2 * g + z), C_BASE % RING, (2 * g + k) * 2 * P + z * P, h_hi, h_lo,
                                         2 * g + k, k == 0, k == 1)
                    mm.then_inc(c_out_full if g < 3 else w_used, 1)

            ffn(0)
            mixer_a()
            ffn(1)
            ffn(2)
            mixer_c()
            ffn(3)
            stat(6)

        @block.vector
        def _(dve):
            steps = [0]

            def mark(ins):
                steps[0] += 1
                ins.then_inc(own, 1)

            def settle():
                dve.wait_ge(own, steps[0])

            def xg(n, m):
                b = A_OUT_BANK[m] if n == 2 else out_bank(m)
                dve.wait_ge(x_new, x_new_count(n, m + 1))
                dve.tensor_scalar(bank(b), x[:, m, :], pcol(PC_G + KD * n + m), None, ALU.mult).then_inc(xg_ready, 1)

            def close_tile(n, m):
                if n in DIRECT_NORMS:
                    dve.wait_ge(x_high, x_low_count(n, m + 1))
                    dve.scalar_tensor_tensor(out=x_lo[:, m, :], in0=x[:, m, :], scalar=pcol(PC_G + KD * n + m),
                                             in1=x_hi[:, m, :].bitcast(F32), op0=ALU.mult,
                                             op1=ALU.subtract).then_inc(x_low, 1)
                elif n in SPLIT_NORMS:
                    b = A_OUT_BANK[m] if n == 2 else out_bank(m)
                    dve.wait_ge(x_high, x_low_count(n, m + 1))
                    dve.tensor_tensor(x_lo[:, m, :], bank(b), x_hi[:, m, :].bitcast(F32), ALU.subtract).then_inc(x_low, 1)
                if m > 0:
                    dve.wait_ge(squared, KD * n + m + 1)
                    if m > 1:
                        dve.wait_ge(sum_step, SUM_STEPS * n + m - 1)
                    dst = square_sum if m == KD - 1 else bank(sum_bank(n))
                    dve.tensor_tensor(dst, bank(sum_bank(n)), squares[:, m % 2, :], ALU.add).then_inc(sum_step, 1)

            def inverse(n, dst):
                dve.wait_ge(rms_ready, n + 1)
                dve.reciprocal(dst, rms).then_inc(r_ready, 1)
                dve.wait_ge(r_ready, n + 1)

            def hidden(f, p, i=0):
                b, z, count = 2 * (p % 4), p % 2, 4 * i + (KF * f + p + 1)
                j = p if isinstance(i, int) else bass.ds(4 * i + p, 1)
                if p % 2 == 0:
                    dve.wait_ge(pair_full, 2 * i + (UNITS * f + p // 2 + 1))
                else:
                    dve.wait_ge(w_used, 4 * i + (FFN_BASE[f] + p + 1))
                dve.tensor_tensor(scaled[:, z, :], bank(b), r[:, :], ALU.mult).then_inc(gate_scaled, 1)
                dve.tensor_tensor(bank(b + 1), bank(b + 1), r[:, :], ALU.mult).then_inc(up_scaled, 1)
                dve.wait_ge(gate_acted, count)
                dve.wait_ge(up_scaled, count)
                dve.tensor_tensor(bank(b), bank(b + 1), acted[:, z, :], ALU.mult).then_inc(hid_ready, 1)
                dve.wait_ge(hid_high, count)
                dve.tensor_tensor(h_lo[:, j, :], bank(b), h_hi[:, j, :].bitcast(F32), ALU.subtract).then_inc(hid_low, 1)

            def ffn(f):
                inverse(FFN_NORM[f], r[:, :])
                with dve.Fori(0, UNITS // 2) as i:
                    for p in range(4):
                        hidden(f, p, i)
                for p in range(4 * (UNITS // 2), KF):
                    hidden(f, p)
                n = NEXT_NORM[f]
                for q in range(QUARTERS):
                    dve.wait_ge(w_used, FFN_BASE[f] + IN_CHUNKS + 4 * (q + 1))
                    for m in (2 * q, 2 * q + 1):
                        dve.scalar_tensor_tensor(out=x[:, m, :], in0=bank(out_bank(m)), scalar=0.5, in1=x[:, m, :],
                                                 op0=ALU.mult, op1=ALU.add).then_inc(x_new, 1)
                        if n in SPLIT_NORMS:
                            xg(n, m)
                    close_tile(n, 2 * q)
                    close_tile(n, 2 * q + 1)

            def glu(v):
                b = 2 * (v % 2)
                dve.wait_ge(w_used, A_BASE + v + 1)
                dve.tensor_tensor(scaled[:, v % 2, :], bank(b + 1), r[:, :], ALU.mult).then_inc(a_gate_scaled, 1)
                mark(dve.tensor_tensor(bank(b), bank(b), r[:, :], ALU.mult))
                dve.wait_ge(a_gate_acted, v + 1)
                settle()
                mark(dve.tensor_tensor(prompt_of(ext_a, v, HA, HA), bank(b, 0, PROMPT), acted[:, v % 2, 0:PROMPT],
                                       ALU.mult))
                dve.tensor_tensor(sample_of(ext_a, v, HA, HA), sample_cols(bank(b, PROMPT, T)),
                                  sample_cols(acted[:, v % 2, PROMPT:T]), ALU.mult).then_inc(a_evacuated, 1)

            def tap_a(i, k):
                n = CONV_STEPS * i + k
                w = pcol(PC_WA + TAPS_A * i + k)
                src, acc = prompt_of(ext_a, i, HA, k), bank(4 + i, k % 2 * PROMPT, (k % 2 + 1) * PROMPT)
                y = y_a[:, i, 0:PROMPT]
                if k == 0:
                    dve.tensor_scalar(acc, src, w, pcol(PC_BA + i), ALU.mult, ALU.add).then_inc(conv_prompt, 1)
                elif k == 1:
                    dve.tensor_scalar(acc, src, w, None, ALU.mult).then_inc(conv_prompt, 1)
                else:
                    dve.wait_ge(conv_prompt, n - 1)
                    dve.scalar_tensor_tensor(out=y if k == TAPS_A - 1 else acc, in0=src, scalar=w,
                                             in1=acc, op0=ALU.mult, op1=ALU.add).then_inc(conv_prompt, 1)
                if k == TAPS_A - 1:
                    dve.wait_ge(conv_prompt, n + 1)
                    dve.tensor_tensor(y, bank(4 + i, PROMPT, 2 * PROMPT), y, ALU.add).then_inc(conv_prompt, 1)

            def sum_taps(i):
                dve.wait_ge(tap_products, i + 1)
                res = y_a[:, i, PROMPT:T]
                dve.tensor_reduce(sample_cols(res), tap_prod, mybir.AxisListType.X, ALU.add).then_inc(conv_sample_sum, 1)
                dve.wait_ge(conv_sample_sum, i + 1)
                dve.tensor_scalar(res, res, pcol(PC_BA + i), None, ALU.add).then_inc(conv_sample, 1)

            def conv_b(v):
                i, b = v - KA, 2 * (v % 2)
                dve.wait_ge(w_used, A_BASE + v + 1)
                mark(dve.tensor_tensor(scaled[:, v % 2, :], bank(b), r[:, :], ALU.mult))
                mark(dve.tensor_tensor(bank(b + 1), bank(b + 1), r[:, :], ALU.mult))
                settle()
                mark(dve.tensor_tensor(prompt_of(ext_b, i, HB, HB), bank(b + 1, 0, PROMPT), scaled[:, v % 2, 0:PROMPT],
                                       ALU.mult))
                mark(dve.tensor_tensor(sample_of(ext_b, i, HB, HB), sample_cols(bank(b + 1, PROMPT, T)),
                                       sample_cols(scaled[:, v % 2, PROMPT:T]), ALU.mult))
                last = sample_cols(bank(b + 1, PROMPT, T))
                for k in range(TAPS_B):
                    settle()
                    w = pcol(PC_WB + TAPS_B * i + k)
                    for src, acc, res in (
                            (prompt_of(ext_b, i, HB, k), bank(b + 1, 0, PROMPT), y_b[:, i, 0:PROMPT]),
                            (sample_of(ext_b, i, HB, k), last,
                             sample_cols(y_b[:, i, PROMPT:T]))):
                        if k == 0:
                            ins = dve.tensor_scalar(acc, src, w, None, ALU.mult)
                        else:
                            ins = dve.scalar_tensor_tensor(out=res if k == TAPS_B - 1 else acc, in0=src, scalar=w,
                                                           in1=acc, op0=ALU.mult, op1=ALU.add)
                        if acc is not last or k < TAPS_B - 1:
                            mark(ins)
                ins.then_inc(a_evacuated, 1)

            def gate_b(v):
                dve.wait_ge(a_evacuated, 2 * KA)
                dve.wait_ge(w_used, A_BASE + v + 1)
                for t in range(2):
                    b, i = 2 * (v % 2) + t, 2 * (v - 2 * KA) + t
                    mark(dve.tensor_tensor(bank(b), bank(b), r[:, :], ALU.mult))
                    settle()
                    dve.tensor_tensor(bank(b), bank(b), y_b[:, i, :], ALU.mult).then_inc(y_ready, 1)
                for t in range(2):
                    b, i = 2 * (v % 2) + t, 2 * (v - 2 * KA) + t
                    dve.wait_ge(y_high, i + 1)
                    ins = dve.tensor_tensor(h_lo[:, KA + i, :], bank(b), h_hi[:, KA + i, :].bitcast(F32), ALU.subtract)
                    ins.then_inc(y_low, 1)

            def mixer_a():
                inverse(1, r[:, :])
                dve.wait_ge(pads_set, 1)
                dve.wait_ge(hist_ab_landed, 16 * 2 * KA)
                taps = [(i, k) for i in range(PE_TILE) for k in range(TAPS_A)]
                for v in range(A_UNITS):
                    (glu if v < KA else conv_b if v < 2 * KA else gate_b)(v)
                    if v in SUM_AT:
                        sum_taps(SUM_AT.index(v))
                    for _ in range(TAPS_BETWEEN[0 if v < KA else 1 if v < 2 * KA else 2]):
                        if taps and taps[0][0] <= v:
                            i, k = taps.pop(0)
                            if k == 0:
                                dve.wait_ge(a_evacuated, i + 1)
                                settle()
                            tap_a(i, k)
                for i, k in taps:
                    if k == 0:
                        dve.wait_ge(a_evacuated, i + 1)
                    tap_a(i, k)
                sum_taps(KA - 1)
                dve.wait_ge(ln_sum_full, 1)
                for i in range(KA):
                    dve.scalar_tensor_tensor(out=y_a[:, i, :], in0=bank(4), scalar=-1.0 / DA, in1=y_a[:, i, :],
                                             op0=ALU.mult, op1=ALU.add).then_inc(ln_centred, 1)
                dve.wait_ge(ln_std_ready, 1)
                mark(dve.reciprocal(bank(6), rms))
                settle()
                for i in range(KA):
                    dve.tensor_tensor(y_a[:, i, :], y_a[:, i, :], bank(6), ALU.mult).then_inc(ln_scaled, 1)
                for i in range(KA):
                    dve.wait_ge(y_high, KA + i + 1)
                    dve.tensor_tensor(h_lo[:, i, :], bank(LN_BANK[i]), h_hi[:, i, :].bitcast(F32),
                                      ALU.subtract).then_inc(y_low, 1)
                def add_out(m):
                    if m % 4 == 3:
                        dve.wait_ge(w_used, A_BASE + A_UNITS + m // 4 * 2 + 2)
                    else:
                        dve.wait_ge(a_out_full, 3 * (m // 4) + m % 4 + 1)
                    dve.tensor_tensor(x[:, m, :], bank(A_OUT_BANK[m]), x[:, m, :], ALU.add).then_inc(x_new, 1)
                    xg(2, m)
                for m in range(KD):
                    add_out(m)
                    if m > 0:
                        close_tile(2, m - 1)
                close_tile(2, KD - 1)

            def mixer_c():
                dve.wait_ge(a_state_out, 16 * 4 * KA)
                mark(dve.memset(ext_c[:, :, 0:HC], 0.0))
                dve.wait_ge(count_set, 1)
                mark(dve.tensor_copy(inv_count[:, 0, :], count_i[:, :]))
                settle()
                for g in (3, 2, 1, 0):
                    mark(dve.tensor_scalar(inv_count[:, g, :], inv_count[:, 0, :], float(WINDOWS[g]), None, ALU.min))
                settle()
                mark(dve.reciprocal(inv_count[:, :, :], inv_count[:, :, :]))
                mark(dve.tensor_tensor(bias_scaled[:, :], par[:, PC_PB:PC_PB + KD], par[:, PC_PS:PC_PS + KD], ALU.mult))
                inverse(4, bank(R_BANK))
                dve.wait_ge(hist_c_landed, 16 * KD)
                settle()

                def normalised(m):
                    g = pcol(PC_G + KD * 4 + m)
                    mark(dve.scalar_tensor_tensor(out=prompt_of(ext_c, m, HC, HC), in0=x[:, m, 0:PROMPT], scalar=g,
                                                  in1=bank(R_BANK, 0, PROMPT), op0=ALU.mult, op1=ALU.mult))
                    dve.scalar_tensor_tensor(out=sample_of(ext_c, m, HC, HC), in0=sample_cols(x[:, m, PROMPT:T]),
                                             scalar=g, in1=sample_cols(bank(R_BANK, PROMPT, T)), op0=ALU.mult,
                                             op1=ALU.mult).then_inc(c_h_ready, 1)

                def pooled_rest(g):
                    for m in (2 * g, 2 * g + 1):
                        dve.wait_ge(pooled_high, m + 1)
                        dve.tensor_tensor(h_lo[:, m, :], bank(m % 2), h_hi[:, m, :].bitcast(F32),
                                          ALU.subtract).then_inc(pooled_low, 1)

                def residual(g):
                    if g < 3:
                        dve.wait_ge(c_out_full, g + 1)
                    else:
                        dve.wait_ge(w_used, C_BASE + 1)
                    for m in (2 * g, 2 * g + 1):
                        dve.wait_ge(x_biased, m + 1)
                        dve.scalar_tensor_tensor(out=x[:, m, :], in0=bank(out_bank(m)), scalar=pcol(PC_PS + m),
                                                 in1=x[:, m, :], op0=ALU.mult, op1=ALU.add).then_inc(x_new, 1)
                    close_tile(5, 2 * g)
                    close_tile(5, 2 * g + 1)

                for g, w in enumerate(WINDOWS):
                    src, tile, n, z = ext_c, slice(2 * g, 2 * g + 2), 1, 0
                    normalised(2 * g)
                    normalised(2 * g + 1)
                    dve.wait_ge(c_h_ready, 2 * g + 2)
                    settle()
                    if g > 0:
                        dve.wait_ge(pooled_ready, 2 * g)
                    while n < w:
                        first = 2 * n - 1
                        mark(dve.tensor_tensor(win[z][:, :, first:ec_w], src[:, tile, first:ec_w],
                                               src[:, tile, first - n:ec_w - n], ALU.add))
                        settle()
                        src, tile, n, z = win[z], slice(0, 2), 2 * n, 1 - z
                    mark(dve.tensor_tensor(head[:, 0, :], src[:, 0, HC:2 * HC], inv_count[:, g, :], ALU.mult))
                    mark(dve.tensor_tensor(head[:, 1, :], src[:, 1, HC:2 * HC], inv_count[:, g, :], ALU.mult))
                    if g > 0:
                        pooled_rest(g - 1)
                        dve.wait_ge(pooled_low, 2 * g)
                    if g > 1:
                        residual(g - 2)
                    settle()
                    for m in (2 * g, 2 * g + 1):
                        b = m % 2
                        mark(dve.tensor_tensor(bank(b, 0, HC), head[:, b, :], ext_c[:, m, HC:2 * HC], ALU.subtract))
                        mark(dve.scalar_tensor_tensor(out=bank(b, HC, PROMPT), in0=src[:, b, 2 * HC:HC + PROMPT],
                                                      scalar=1.0 / w, in1=ext_c[:, m, 2 * HC:HC + PROMPT],
                                                      op0=ALU.mult, op1=ALU.subtract))
                        dve.scalar_tensor_tensor(out=sample_cols(bank(b, PROMPT, T)), in0=sample_of(src, b, HC, HC),
                                                 scalar=1.0 / w, in1=sample_of(ext_c, m, HC, HC),
                                                 op0=ALU.mult, op1=ALU.subtract).then_inc(pooled_ready, 1)
                pooled_rest(3)
                residual(2)
                residual(3)

            def final():
                inverse(6, bank(R_BANK))
                dve.wait_ge(c_state_out, 16 * 2 * KD)
                for m in range(KD):
                    dve.scalar_tensor_tensor(out=y_out[:, m, :], in0=x[:, m, :], scalar=pcol(PC_G + KD * 6 + m),
                                             in1=bank(R_BANK), op0=ALU.mult, op1=ALU.mult).then_inc(y_done, 1)

            dve.wait_ge(par_landed, 16)
            for m in range(KD):
                close_tile(0, m)
            ffn(0)
            mixer_a()
            ffn(1)
            ffn(2)
            mixer_c()
            ffn(3)
            final()


TAPS_BETWEEN = (10, 6, 8)
PE_TILE = KA - 1
PE_COLS = PC_WA + TAPS_A * PE_TILE
DIAGS_AT_ONCE = 5
CONV_STEPS = TAPS_A + 1
SUM_AT = (4, 6, 8)
ROW_AT = 9
PRODUCTS_AT = (6, 8, 10, 12)

INPUTS = {
    "x_t": (P, KD, T), "par": (P, PARAMS), "hist_a": (P, KA, SEQS, HA), "hist_b": (P, KA, SEQS, HB),
    "hist_c": (P, KD, SEQS, HC), "ffn_w_in": (2, 2, D, 2 * DFF), "ffn_w_out": (2, 2, DFF, D),
    "mix_w_in": (1, D, 5 * DA), "mix_w_out": (1, D, D), "pool_w": (1, 4, 256, 256),
}
OUTPUTS = {
    "y_t": (P, KD, T), "new_a_prompt": (P, KA, HA), "new_a_sample": (P, KA, SEQS, HA),
    "new_b_prompt": (P, KA, HB), "new_b_sample": (P, KA, SEQS, HB),
    "new_c_prompt": (P, KD, HC), "new_c_sample": (P, KD, SEQS, HC),
}


def kernel(**inputs):
    import numpy as np
    from concourse import bacc
    from concourse.bass_utils import run_bass_kernel_spmd

    g = {k: np.asarray(v) for k, v in inputs.items()}

    def by_partition(v):
        v = v.reshape(*v.shape[:-1], v.shape[-1] // P, P)
        return np.moveaxis(v, -1, 0)

    tokens = np.concatenate([g["x_prompt"].reshape(PROMPT, D), g["x_sample"].reshape(SEQS * STEP, D)])
    par = np.concatenate([
        by_partition(g["norm_g"]).reshape(P, 6 * KD),
        by_partition(g["final_norm_g"]),
        by_partition(g["conv_a_w"][0]).transpose(0, 2, 1).reshape(P, KA * TAPS_A),
        by_partition(g["conv_a_b"][0]), by_partition(g["ln_a_g"][0]), by_partition(g["ln_a_b"][0]),
        by_partition(g["conv_b_w"][0]).transpose(0, 2, 1).reshape(P, KA * TAPS_B),
        by_partition(g["pool_b"][0]), by_partition(g["pool_scale"][0]),
    ], axis=1)

    def history(v):
        return by_partition(v).transpose(0, 3, 1, 2)

    data = {
        "x_t": by_partition(tokens).transpose(0, 2, 1), "par": par,
        "hist_a": history(g["state_conv_a"][0]), "hist_b": history(g["state_conv_b"][0]),
        "hist_c": history(g["state_pool"][0]),
        "ffn_w_in": g["ffn_w_in"], "ffn_w_out": g["ffn_w_out"], "mix_w_in": g["mix_w_in"],
        "mix_w_out": g["mix_w_out"], "pool_w": g["pool_w"],
    }
    data = {k: np.ascontiguousarray(v) for k, v in data.items()}

    nc = bacc.Bacc("TRN2", target_bir_lowering=False, num_devices=1)
    aps = {k: nc.dram_tensor(k, s, F32, kind="ExternalInput").ap() for k, s in INPUTS.items()}
    aps |= {k: nc.dram_tensor(k, s, F32, kind="ExternalOutput").ap() for k, s in OUTPUTS.items()}
    build(nc, aps)
    got = run_bass_kernel_spmd(nc, [data], core_ids=[0]).results[0]

    y = got["y_t"].transpose(2, 1, 0).reshape(T, D)

    def prompt_rows(v):
        return np.ascontiguousarray(v.transpose(2, 1, 0).reshape(1, 1, v.shape[2], -1))

    def sample_rows(v):
        return np.ascontiguousarray(v.transpose(2, 3, 1, 0).reshape(1, SEQS, v.shape[3], -1))

    return (np.ascontiguousarray(y[:PROMPT].reshape(1, PROMPT, D)),
            np.ascontiguousarray(y[PROMPT:].reshape(SEQS, STEP, D)),
            prompt_rows(got["new_a_prompt"]), prompt_rows(got["new_b_prompt"]), prompt_rows(got["new_c_prompt"]),
            sample_rows(got["new_a_sample"]), sample_rows(got["new_b_sample"]), sample_rows(got["new_c_sample"]))
```

```python
from contextlib import ExitStack

import concourse.bass as bass
from concourse import mybir

F32 = mybir.dt.float32
F32R = mybir.dt.float32r
ALU = mybir.AluOpType
ACT = mybir.ActivationFunctionType

P = 128
PROMPT, SEQS, STEP = 256, 8, 4
T = PROMPT + SEQS * STEP
D = 1024
KD = D // P
DFF = 2816
KF = DFF // P
DA = 512
KA = DA // P
TAPS_A, TAPS_B = 31, 3
HA, HB, HC = TAPS_A - 1, TAPS_B - 1, 15
WINDOWS = (2, 4, 8, 16)
EPS = 1e-6

RING, SLOT = 4, 2048
UNITS = KF // 2
IN_CHUNKS = 2 * UNITS
QUARTERS = 4
Q_SPLIT = ((0, 6), (6, 12), (12, 18), (18, 22))
OUT_CHUNKS = QUARTERS * len(Q_SPLIT)
FFN_CHUNKS = IN_CHUNKS + OUT_CHUNKS
A_UNITS = 10
A_CHUNKS = A_UNITS + 4
FFN_BASE = (0, FFN_CHUNKS + A_CHUNKS, 2 * FFN_CHUNKS + A_CHUNKS, 3 * FFN_CHUNKS + A_CHUNKS + 1)
A_BASE = FFN_CHUNKS
C_BASE = 3 * FFN_CHUNKS + A_CHUNKS
CHUNKS = C_BASE + 1 + FFN_CHUNKS

SPLIT_NORMS = (0, 1, 2, 3, 4, 5)
FFN_NORM = (0, 2, 3, 5)
NEXT_NORM = (1, 3, 4, 6)

FIRST_IN = 3 * (((0, 0), (1, 0), (0, 1), (1, 1)),) + (((0, 0), (0, 1), (1, 0), (1, 1)),)

LATE_NORMS = (4, 6)


def sum_steps(n, tiles=1):
    full = [KD - 2 if k in LATE_NORMS else KD - 1 for k in range(n + 1)]
    return sum(full[:n]) + min(tiles - 1, full[n])


A_OUT_BANK = (3, 0, 1, 2, 4, 5, 6, 7)
C_BANK = (0, 1, 2, 3, 5, 6, 7, 4)

PC_G, PC_WA, PC_BA, PC_LG, PC_LB, PC_WB, PC_PB, PC_PS = 0, 56, 180, 184, 188, 192, 204, 212
PARAMS = 220


def sum_bank(n):
    return 3 if n > 0 else 5


def stat_bank(n):
    return 4 if n != 5 else 7


def out_bank(m):
    return 4 + m % 4


def build(nc, a):
    ctx = ExitStack()
    with ctx:
        def sb(name, shape, dt=F32):
            return ctx.enter_context(nc.sbuf_tensor(name, shape, dt))

        def sem(name):
            return ctx.enter_context(nc.semaphore(name))

        w_raw = sb("w_raw", [P, RING, SLOT])
        w_hi = sb("w_hi", [P, RING, SLOT], F32R)
        w_lo = sb("w_lo", [P, RING, SLOT], F32R)
        x = sb("x", [P, KD, T])
        x_hi = sb("x_hi", [P, KD, T], F32R)
        x_lo = sb("x_lo", [P, KD, T], F32R)
        h_hi = sb("h_hi", [P, KF, T], F32R)
        h_lo = sb("h_lo", [P, KF, T], F32R)
        gate_buf = sb("gate_buf", [P, 4, T])
        scaled, acted = gate_buf[:, 0:2, :], gate_buf[:, 2:4, :]
        norm_buf = sb("norm_buf", [P, 4, T])
        squares, rms, square_sum = norm_buf[:, 0:2, :], norm_buf[:, 2, :], norm_buf[:, 3, :]
        r = sb("r", [P, T])
        ones = sb("ones", [P, P])
        ident = sb("ident", [P, P])
        taps_hi = sb("taps_hi", [P, TAPS_A], F32R)
        taps_lo = sb("taps_lo", [P, TAPS_A])
        eps = sb("eps", [P, 1])
        primed = sb("primed", [P, 1])
        par = sb("par_sb", [P, PARAMS])
        bias_scaled = sb("bias_scaled", [P, KD])
        count_i = sb("count_i", [P, HC], mybir.dt.int32)
        inv_count = sb("inv_count", [P, len(WINDOWS), HC])
        head = sb("head", [P, 2, HC])
        mix = sb("mix", [P, 5760])
        psum = ctx.enter_context(nc.psum_tensor("psum", [P, 8, 512], F32))

        ea_w, eb_w = HA + PROMPT + SEQS * (HA + STEP), HB + PROMPT + SEQS * (HB + STEP)
        ext_a = mix[:, 0:KA * ea_w].rearrange("p (i n) -> p i n", i=KA)
        eb0 = KA * ea_w
        ext_b = mix[:, eb0:eb0 + KA * eb_w].rearrange("p (i n) -> p i n", i=KA)
        y0 = eb0 + KA * eb_w
        y_a = mix[:, y0:y0 + KA * T].rearrange("p (i n) -> p i n", i=KA)
        y_b = mix[:, y0 + KA * T:y0 + 2 * KA * T].rearrange("p (i n) -> p i n", i=KA)
        ln_sq = y_b
        inverse_std = square_sum
        row_hi, row_lo = (h[:, 0:2, :].rearrange("p a b -> p (a b)")[:, 0:HA + PROMPT] for h in (h_hi, h_lo))
        diag_hi, diag_lo = (
            h[:, KD:KF, :].rearrange("p a b -> p (a b)")[:, 0:TAPS_A * P].rearrange("p (k n) -> p k n", k=TAPS_A)
            for h in (h_hi, h_lo))
        n_prod = SEQS * STEP * TAPS_A
        tap_prod = norm_buf[:, :, :].rearrange("p a b -> p (a b)")[:, 0:n_prod].rearrange(
            "p (s t k) -> p s t k", s=SEQS, t=STEP)
        n_hist = SEQS * HC
        n_tail = HC + SEQS * STEP
        ec_w = HC + PROMPT + SEQS * (HC + STEP)
        taken = [0]

        def of_mix(tiles, n):
            taken[0] += tiles * n
            return mix[:, taken[0] - tiles * n:taken[0]].rearrange("p (i n) -> p i n", i=tiles)

        state_c = of_mix(KD, SEQS * (HC + STEP)).rearrange("p i (s n) -> p (i s) n", s=SEQS)
        prompt_tail = of_mix(KD, HC)
        xg_tail = of_mix(KD, n_tail)
        y_out = mix[:, taken[0]:taken[0] + KD * T].rearrange("p (i n) -> p i n", i=KD)
        ext_c = of_mix(KD, ec_w)
        c_squares = of_mix(2, T)
        c_square = [c_squares[:, m % 2, :] for m in range(4)] + [norm_buf[:, m, :] for m in range(4)]
        win = [buf[:, :, :].rearrange("p a b -> p (a b)")[:, 0:2 * ec_w].rearrange("p (i n) -> p i n", i=2)
               for buf in (gate_buf, norm_buf)]
        ext_pair = [ext_c[:, 2 * g:2 * g + 2, :] for g in range(4)]
        win_raw = w_raw[:, C_BASE % RING, 0:2 * ec_w].rearrange("p (i n) -> p i n", i=2)
        pool_win = {1: (win[1], win_raw), 3: (ext_pair[0], ext_pair[1], ext_pair[0], ext_pair[1])}

        def prompt_of(ext, i, hist, at, n=PROMPT):
            return ext[:, i, at:at + n]

        def sample_of(ext, i, hist, at, n=STEP):
            s = ext[:, i, hist + PROMPT:hist + PROMPT + SEQS * (hist + STEP)]
            return s.rearrange("p (s n) -> p s n", s=SEQS)[:, :, at:at + n]

        def bank(b, lo=0, hi=T):
            return psum[:, b, lo:hi]

        def sample_cols(ap):
            return ap.rearrange("p (s n) -> p s n", s=SEQS)

        def pcol(c):
            return par[:, c:c + 1]

        w_landed = [sem(f"w_landed{i}") for i in range(RING)]
        w_high = sem("w_high")
        w_low = sem("w_low")
        w_used = sem("w_used")
        w_first = [sem(f"w_first{i}") for i in range(RING)]
        first_high = sem("first_high")
        first_low = sem("first_low")
        x_landed = [sem(f"x_landed{i}") for i in range(KD // 2)]
        par_landed = sem("par_landed")
        hist_ab_landed = sem("hist_ab_landed")
        hist_c_landed = sem("hist_c_landed")
        consts_set = sem("consts_set")
        pads_set = sem("pads_set")
        count_set = sem("count_set")
        x_new = sem("x_new")
        x_high = sem("x_high")
        x_low = sem("x_low")
        squared = sem("squared")
        sum_step = sem("sum_step")
        stat_full = sem("stat_full")
        rms_ready = sem("rms_ready")
        r_ready = sem("r_ready")
        pair_full = sem("pair_full")
        gate_scaled = sem("gate_scaled")
        up_scaled = sem("up_scaled")
        gate_acted = sem("gate_acted")
        hid_ready = sem("hid_ready")
        hid_high = sem("hid_high")
        out_full = sem("out_full")
        hid_low = sem("hid_low")
        a_gate_scaled = sem("a_gate_scaled")
        a_gate_acted = sem("a_gate_acted")
        a_evacuated = sem("a_evacuated")
        conv_prompt = sem("conv_prompt")
        tap_products = sem("tap_products")
        taps_high = sem("taps_high")
        taps_low = sem("taps_low")
        diag_ready = sem("diag_ready")
        row_high = sem("row_high")
        row_low = sem("row_low")
        conv_pe_full = sem("conv_pe_full")
        conv_pe_ready = sem("conv_pe_ready")
        ident_zero = sem("ident_zero")
        ident_set = sem("ident_set")
        conv_sample_sum = sem("conv_sample_sum")
        conv_sample = sem("conv_sample")
        prime_done = sem("prime_done")
        y_ready = sem("y_ready")
        y_high = sem("y_high")
        y_low = sem("y_low")
        ln_sum_full = sem("ln_sum_full")
        ln_centred = sem("ln_centred")
        ln_squared = sem("ln_squared")
        ln_var_full = sem("ln_var_full")
        ln_std_ready = sem("ln_std_ready")
        ln_scaled = sem("ln_scaled")
        a_out_full = sem("a_out_full")
        a_state_out = sem("a_state_out")
        c_full = sem("c_full")
        c_hist_ready = sem("c_hist_ready")
        c_evacuated = sem("c_evacuated")
        window_step = sem("window_step")
        square_added = sem("square_added")
        tail_ready = sem("tail_ready")
        state_ready = sem("state_ready")
        c_state_out = sem("c_state_out")
        y_times_g = sem("y_times_g")
        half_r = sem("half_r")
        y_done = sem("y_done")
        y_pool = sem("y_pool")
        out_stored = sem("out_stored")
        own = sem("own")

        block = ctx.enter_context(nc.Block())

        def x_low_count(n, tiles):
            return KD * SPLIT_NORMS.index(n) + tiles

        def x_new_count(n, tiles):
            return KD * (n - 1) + tiles

        def y_part(y, part, half):
            return y[:, 4 * part:4 * part + 4, half * T // 2:(half + 1) * T // 2]

        def times_r(engine, part, half):
            y = y_part(y_out, part, half)
            by = r[:, half * T // 2:(half + 1) * T // 2].unsqueeze(1).broadcast_to([P, 4, T // 2])
            return engine.tensor_tensor(y, y, by, ALU.mult)

        @block.sync
        def _(sp):
            def slot_free(c, more=0):
                sp.wait_ge(w_low, c - RING + 1 + more)
                if c == C_BASE + RING:
                    sp.wait_ge(x_new, x_new_count(5, 4))

            def load(c, dst0, src0, dst1, src1):
                sp.dma_start(dst0, src0).then_inc(w_landed[c % RING], 16)
                sp.dma_start(dst1, src1).then_inc(w_landed[c % RING], 16)

            def load_in(f, c, half, unit):
                w = a["ffn_w_in"][f // 2, f % 2].rearrange("(k p) (g n) -> p k g n", p=P, g=2)
                dst = w_raw[:, c % RING, :].rearrange("p (k g n) -> p k g n", k=4, g=2)
                k = slice(4 * half, 4 * half + 4)
                cols = bass.ds(unit * 2 * P, 2 * P)
                load(c, dst[:, :, 0, :], w[:, k, 0, cols], dst[:, :, 1, :], w[:, k, 1, cols])

            def first_loads():
                w = a["ffn_w_in"][0, 0].rearrange("(k p) (g n) -> p k g n", p=P, g=2)

                def weights(c, part):
                    half, unit = FIRST_IN[0][c]
                    dst = w_raw[:, c, :].rearrange("p (k g n) -> p k g n", k=4, g=2)
                    k, from_k = slice(2 * part, 2 * part + 2), slice(4 * half + 2 * part, 4 * half + 2 * part + 2)
                    for g in range(2):
                        sp.dma_start(dst[:, k, g, :], w[:, from_k, g, unit * 2 * P:(unit + 1) * 2 * P]).then_inc(
                            (w_landed if part else w_first)[c], 16)

                def tokens(pair):
                    tiles = slice(2 * pair, 2 * pair + 2)
                    sp.dma_start(x[:, tiles, :], a["x_t"][:, tiles, :]).then_inc(x_landed[pair], 16)

                weights(0, 0)
                tokens(0)
                weights(0, 1)
                tokens(1)
                tokens(2)
                weights(1, 0)
                tokens(3)
                weights(1, 1)
                for c in range(2, RING):
                    weights(c, 0)
                    weights(c, 1)

            def load_out(f, c, part, quarter):
                w = a["ffn_w_out"][f // 2, f % 2].rearrange("(k p) n -> p k n", p=P)
                k0, k1 = Q_SPLIT[part]
                km = (k0 + k1) // 2
                dst = w_raw[:, c % RING, 0:(k1 - k0) * 2 * P].rearrange("p (k n) -> p k n", n=2 * P)
                cols = bass.ds(quarter * 2 * P, 2 * P)
                load(c, dst[:, 0:km - k0, :], w[:, k0:km, cols], dst[:, km - k0:k1 - k0, :], w[:, km:k1, cols])

            def ffn(f, small):
                base = FFN_BASE[f]
                if f == 0:
                    first_loads()
                for j in range(RING if f == 0 else 0, RING):
                    slot_free(base + j)
                    load_in(f, base + j, *FIRST_IN[f][j])
                if f < 3:
                    small()
                with sp.Fori(0, UNITS // 2 - 1) as i:
                    for j in range(RING, 2 * RING):
                        slot_free(base + j, 4 * i)
                        load_in(f, base + j, j % 2, 2 * i + j // 2)
                for j in range(4 * (UNITS // 2), IN_CHUNKS):
                    slot_free(base + j)
                    load_in(f, base + j, j % 2, j // 2)
                if f == 3:
                    small()
                base += IN_CHUNKS
                with sp.Fori(0, QUARTERS) as q:
                    for j in range(RING):
                        slot_free(base + j, 4 * q)
                        load_out(f, base + j, j, q)

            def mixer_a():
                w = a["mix_w_in"][0].rearrange("(k p) n -> p k n", p=P)
                for v in range(A_UNITS):
                    c = A_BASE + v
                    slot_free(c)
                    dst = w_raw[:, c % RING, :].rearrange("p (k g n) -> p k g n", k=KD, g=2)
                    if v < 2 * KA:
                        c0 = (0 if v < KA else 3 * DA) + v % KA * P
                        load(c, dst[:, :, 0, :], w[:, :, c0:c0 + P], dst[:, :, 1, :], w[:, :, c0 + DA:c0 + DA + P])
                    else:
                        c0 = 2 * DA + (v - 2 * KA) * 2 * P
                        dst = w_raw[:, c % RING, :].rearrange("p (k n) -> p k n", k=KD)
                        load(c, dst[:, 0:4, :], w[:, 0:4, c0:c0 + 2 * P], dst[:, 4:8, :], w[:, 4:8, c0:c0 + 2 * P])
                w = a["mix_w_out"][0].rearrange("(k p) n -> p k n", p=P)
                for o in range(4):
                    c = A_BASE + A_UNITS + o
                    slot_free(c)
                    k0, c0 = (KA, 0)[o % 2], o // 2 * 512
                    dst = w_raw[:, c % RING, :].rearrange("p (k n) -> p k n", k=KA)
                    load(c, dst[:, 0:2, :], w[:, k0:k0 + 2, c0:c0 + 512],
                         dst[:, 2:4, :], w[:, k0 + 2:k0 + 4, c0:c0 + 512])

            def mixer_c():
                slot_free(C_BASE)
                w = a["pool_w"][0].rearrange("g (k p) n -> p (g k) n", p=P)
                dst = w_raw[:, C_BASE % RING, :].rearrange("p (k n) -> p k n", k=KD)
                load(C_BASE, dst[:, 0:4, :], w[:, 0:4, :], dst[:, 4:8, :], w[:, 4:8, :])

            def history_ab():
                for i in range(KA):
                    sp.dma_start(sample_of(ext_a, i, HA, 0, HA), a["hist_a"][:, i, :, :]).then_inc(hist_ab_landed, 16)
                    sp.dma_start(sample_of(ext_b, i, HB, 0, HB), a["hist_b"][:, i, :, :]).then_inc(hist_ab_landed, 16)

            def mixer_a_state():
                sp.wait_ge(a_evacuated, 2 * KA)
                sp.wait_ge(hist_ab_landed, 16 * 2 * KA)
                for i in range(KA):
                    sp.dma_start(a["new_a_prompt"][:, i, :], ext_a[:, i, PROMPT:PROMPT + HA]).then_inc(a_state_out, 16)
                    sp.dma_start(a["new_a_sample"][:, i, :, :], sample_of(ext_a, i, HA, STEP, HA)).then_inc(a_state_out, 16)
                    sp.dma_start(a["new_b_prompt"][:, i, :], ext_b[:, i, PROMPT:PROMPT + HB]).then_inc(a_state_out, 16)
                    sp.dma_start(a["new_b_sample"][:, i, :, :], sample_of(ext_b, i, HB, STEP, HB)).then_inc(a_state_out, 16)

            def history_c():
                sp.wait_ge(a_state_out, 16 * 4 * KA)
                sp.wait_ge(y_low, KD)
                sp.dma_start(state_c[:, :, 0:HC], a["hist_c"].rearrange("p i s n -> p (i s) n")).then_inc(hist_c_landed, 16)

            def mixer_c_state():
                sp.wait_ge(state_ready, 2)
                sp.dma_start(a["new_c_prompt"], prompt_tail).then_inc(c_state_out, 16)
                sp.dma_start(a["new_c_sample"].rearrange("p i s n -> p (i s) n"),
                             state_c[:, :, STEP:HC + STEP]).then_inc(c_state_out, 16)

            ffn(0, history_ab)
            mixer_a()
            ffn(1, mixer_a_state)
            ffn(2, history_c)
            mixer_c()
            ffn(3, mixer_c_state)
            sp.wait_ge(c_state_out, 32)
            for part, half, done, count in ((0, 0, y_done, 1), (1, 0, y_pool, 1), (0, 1, y_done, 2), (1, 1, y_done, 3)):
                sp.wait_ge(done, count)
                sp.dma_start(y_part(a["y_t"], part, half), y_part(y_out, part, half)).then_inc(out_stored, 16)
            sp.wait_ge(out_stored, 16 * KD // 2)

        @block.gpsimd
        def _(pool):
            pool.memset(ones[:, :], 1.0)
            pool.memset(eps[:, :], EPS).then_inc(consts_set, 1)
            pool.memset(ext_a[:, :, 0:HA], 0.0)
            pool.memset(ext_b[:, :, 0:HB], 0.0).then_inc(pads_set, 1)
            pool.iota(count_i[:, :], pattern=[[1, HC]], base=1, channel_multiplier=0).then_inc(count_set, 1)

            def low(c, n, more=0):
                pool.wait_ge(w_high, c + 1 + more)
                s = c % RING
                pool.tensor_tensor(w_lo[:, s, 0:n], w_raw[:, s, 0:n], w_hi[:, s, 0:n].bitcast(F32),
                                   ALU.subtract).then_inc(w_low, 1)

            pool.memset(ident[:, :], 0.0).then_inc(ident_zero, 1)
            pool.wait_ge(ident_zero, 1)
            pool.affine_select(out=ident[:, :], in_=ident[:, :], compare_op=ALU.not_equal, fill=1.0, base=0,
                               pattern=[[-1, P]], channel_multiplier=1).then_inc(ident_set, 1)

            def first(c):
                for k in range(4):
                    if k < 3:
                        pool.wait_ge(first_high, 3 * c + k + 1)
                    else:
                        pool.wait_ge(w_high, c + 1)
                    cols = slice(k * 4 * P, (k + 1) * 4 * P)
                    pool.tensor_tensor(w_lo[:, c, cols], w_raw[:, c, cols], w_hi[:, c, cols].bitcast(F32),
                                       ALU.subtract).then_inc(first_low if k < 3 else w_low, 1)

            def ffn(f):
                base = FFN_BASE[f]
                for j in range(RING):
                    if f == 3 and j == 2:
                        windows(1)
                    if f == 0:
                        first(j)
                    else:
                        low(base + j, SLOT)
                    if f == 3 and j == 2:
                        windows(3)
                        new_state_c()
                with pool.Fori(0, UNITS // 2 - 1) as i:
                    for j in range(RING, 2 * RING):
                        low(base + j, SLOT, 4 * i)
                for j in range(4 * (UNITS // 2), IN_CHUNKS):
                    low(base + j, SLOT)
                base += IN_CHUNKS
                with pool.Fori(0, QUARTERS) as q:
                    for j in range(RING):
                        low(base + j, (Q_SPLIT[j][1] - Q_SPLIT[j][0]) * 2 * P, 4 * q)

            def windows(g):
                pool.wait_ge(c_evacuated, 4 if g == 1 else 6)
                pool.wait_ge(c_hist_ready, 2 * g + 2)
                src, n, before = ext_pair[g], 1, 0 if g == 1 else 2
                for step, dst in enumerate(pool_win[g]):
                    if step > 0:
                        pool.wait_ge(window_step, before + step)
                    if dst is win_raw:
                        pool.wait_ge(w_used, C_BASE + 1)
                    if g == 3 and step < 2:
                        pool.wait_ge(x_new, x_new_count(5, 2 * step + 2))
                    first = 2 * n - 1
                    pool.tensor_tensor(dst[:, :, first:ec_w], src[:, :, first:ec_w], src[:, :, first - n:ec_w - n],
                                       ALU.add).then_inc(window_step, 1)
                    src, n = dst, 2 * n

            def new_state_c():
                pool.wait_ge(tail_ready, KD)
                pool.wait_ge(r_ready, 5)
                pool.wait_ge(hist_c_landed, 16)
                tail_r = r[:, PROMPT - HC:PROMPT].unsqueeze(1).broadcast_to([P, KD, HC])
                pool.tensor_tensor(prompt_tail, xg_tail[:, :, 0:HC], tail_r, ALU.mult).then_inc(state_ready, 1)
                sample_r = sample_cols(r[:, PROMPT:T]).unsqueeze(1).broadcast_to([P, KD, SEQS, STEP])
                pool.tensor_tensor(state_c[:, :, HC:HC + STEP].rearrange("p (i s) n -> p i s n", s=SEQS),
                                   xg_tail[:, :, HC:n_tail].rearrange("p i (s n) -> p i s n", s=SEQS),
                                   sample_r, ALU.mult).then_inc(state_ready, 1)

            def tap_product(i):
                pool.wait_ge(a_evacuated, i + 1)
                if i == 0:
                    pool.wait_ge(par_landed, 16)
                    pool.wait_ge(hist_ab_landed, 16 * 2 * KA)
                else:
                    pool.wait_ge(conv_sample_sum, i)
                row = sample_of(ext_a, i, HA, 0)
                under = bass.AP(row.tensor, row.offset, [[5760, P], [HA + STEP, SEQS], [1, STEP], [1, TAPS_A]])
                taps = par[:, PC_WA + TAPS_A * i:PC_WA + TAPS_A * (i + 1)]
                taps = taps.unsqueeze(1).unsqueeze(1).broadcast_to([P, SEQS, STEP, TAPS_A])
                pool.tensor_tensor(tap_prod, under, taps, ALU.mult).then_inc(tap_products, 1)

            ffn(0)
            for c in range(A_BASE, A_BASE + A_CHUNKS):
                low(c, SLOT)
                if c == A_BASE:
                    pool.wait_ge(taps_high, 1)
                    pool.tensor_tensor(taps_lo[:, :], par[:, PE_COLS:PE_COLS + TAPS_A], taps_hi[:, :].bitcast(F32),
                                       ALU.subtract).then_inc(taps_low, 1)
                if c - A_BASE == ROW_AT:
                    pool.wait_ge(row_high, 1)
                    pool.tensor_tensor(row_lo, ext_a[:, PE_TILE, 0:HA + PROMPT], row_hi.bitcast(F32),
                                       ALU.subtract).then_inc(row_low, 1)
                if c - A_BASE in PRODUCTS_AT:
                    tap_product(PRODUCTS_AT.index(c - A_BASE))
            ffn(1)
            ffn(2)
            low(C_BASE, SLOT)
            ffn(3)
            pool.wait_ge(y_times_g, KD)
            pool.wait_ge(half_r, 1)
            times_r(pool, 1, 0).then_inc(y_pool, 1)

        def chunk_cols(c):
            for base in FFN_BASE:
                if base + IN_CHUNKS <= c < base + FFN_CHUNKS:
                    k0, k1 = Q_SPLIT[(c - base - IN_CHUNKS) % 4]
                    return (k1 - k0) * 2 * P
            return SLOT

        @block.scalar
        def _(act):
            def high(c, i=None):
                if c >= CHUNKS:
                    return
                more = 0 if i is None else i
                n = chunk_cols(c)
                act.wait_ge(w_landed[c % RING], 32 * (c // RING + 1) + 32 * more)
                if c >= RING:
                    act.wait_ge(w_used, c - RING + 1 + RING * more)
                act.activation(w_hi[:, c % RING, 0:n], w_raw[:, c % RING, 0:n], ACT.Copy).then_inc(w_high, 1)

            def high_part(n, m):
                if n == 0:
                    act.wait_ge(x_landed[m // 2], 16)
                else:
                    act.wait_ge(x_new, x_new_count(n, m + 1))
                act.activation(x_hi[:, m, :], x[:, m, :], ACT.Copy, scale=pcol(PC_G + KD * n + m)).then_inc(x_high, 1)

            def square(n, m):
                if n > 0:
                    act.wait_ge(x_new, x_new_count(n, m + 1))
                if n == 5:
                    if m in (2, 3):
                        act.wait_ge(square_added, m - 1)
                    dst = c_square[m]
                else:
                    if m >= 3:
                        act.wait_ge(sum_step, sum_steps(n, m - 1))
                    dst = bank(sum_bank(n)) if m == 0 else squares[:, m % 2, :]
                act.activation(dst, x[:, m, :], ACT.Square).then_inc(squared, 1)

            def norm_tile(n, m):
                if n in SPLIT_NORMS:
                    high_part(n, m)
                square(n, m)

            def times_g(m):
                act.activation(y_out[:, m, :], x[:, m, :], ACT.Copy, scale=pcol(PC_G + KD * 6 + m)).then_inc(y_times_g, 1)

            def tail(m):
                act.activation(xg_tail[:, m, :], x[:, m, PROMPT - HC:T], ACT.Copy,
                               scale=pcol(PC_G + KD * 4 + m)).then_inc(tail_ready, 1)

            primes = [0]

            def prime(func):
                if primes[0]:
                    act.wait_ge(prime_done, primes[0])
                primes[0] += 1
                act.activation(primed[:, :], eps[:, :], func).then_inc(prime_done, 1)

            def root(n):
                act.wait_ge(stat_full, n + 1)
                act.activation(rms, bank(stat_bank(n)), ACT.Sqrt, bias=eps[:, :],
                               scale=1.0 / D).then_inc(rms_ready, 1)

            def hidden(f, b, z, j, pairs_before):
                act.wait_ge(gate_scaled, pairs_before + 1)
                act.activation(acted[:, z, :], scaled[:, z, :], ACT.Silu).then_inc(gate_acted, 1)
                act.wait_ge(hid_ready, pairs_before + 1)
                act.activation(h_hi[:, j, :], bank(b), ACT.Copy).then_inc(hid_high, 1)

            def hidden_at(f, p, i=None):
                b = 4 * (p // 2 % 2) + 2 * (p % 2)
                if i is None:
                    hidden(f, b, p % 2, p, KF * f + p)
                else:
                    hidden(f, b, p % 2, bass.ds(4 * i + p, 1), 4 * i + (KF * f + p))

            def ffn(f):
                base = FFN_BASE[f]
                if f > 0:
                    root(FFN_NORM[f])
                prime(ACT.Silu)
                high(base + RING)
                hidden_at(f, 0)
                hidden_at(f, 1)
                high(base + RING + 1)
                for p in range(2, 4):
                    high(base + RING + p)
                    hidden_at(f, p)
                with act.Fori(0, 3) as i:
                    for p in range(4, 8):
                        high(base + RING + p, i)
                        hidden_at(f, p, i)
                for p in range(16, IN_CHUNKS):
                    high(base + RING + p)
                    hidden_at(f, p)
                base += IN_CHUNKS
                prime(ACT.Sqrt)
                for q in range(QUARTERS):
                    for j in range(3):
                        high(base + 4 * q + j + RING)
                    tiles = (2 * q, 2 * q + 1)
                    if NEXT_NORM[f] == 4:
                        for m in tiles:
                            square(4, m)
                        for m in tiles:
                            high_part(4, m)
                        for m in tiles:
                            tail(m)
                    else:
                        for m in tiles:
                            norm_tile(NEXT_NORM[f], m)
                            if NEXT_NORM[f] == 6 and q < QUARTERS - 1:
                                times_g(m)
                    if q == QUARTERS - 1 and NEXT_NORM[f] in (4, 6):
                        root(NEXT_NORM[f])
                    if q < QUARTERS - 1 or NEXT_NORM[f] != 4:
                        high(base + 4 * q + 3 + RING)

            def split_y(k, src):
                act.activation(h_hi[:, k, :], src, ACT.Copy).then_inc(y_high, 1)

            def mixer_a():
                root(1)
                prime(ACT.Sigmoid)
                high(A_BASE + RING)
                for v in range(A_UNITS):
                    if v > 0:
                        high(A_BASE + RING + v)
                    if v < KA:
                        act.wait_ge(a_gate_scaled, v + 1)
                        act.activation(acted[:, v % 2, :], scaled[:, v % 2, :], ACT.Sigmoid).then_inc(a_gate_acted, 1)
                    elif v >= 2 * KA:
                        for t in range(2):
                            i = 2 * (v - 2 * KA) + t
                            act.wait_ge(y_ready, i + 1)
                            split_y(KA + i, bank(2 * (v % 2) + t))
                    if v == KA:
                        act.wait_ge(a_evacuated, KA)
                        act.wait_ge(hist_ab_landed, 16 * 2 * KA)
                        act.wait_ge(pads_set, 1)
                        act.activation(row_hi, ext_a[:, PE_TILE, 0:HA + PROMPT], ACT.Copy).then_inc(row_high, 1)
                    if v == 0:
                        act.wait_ge(taps_low, 1)
                        act.wait_ge(taps_high, 1)
                        act.wait_ge(ident_set, 1)
                    for k in range(DIAGS_AT_ONCE * v, min(DIAGS_AT_ONCE * (v + 1), TAPS_A)):
                        act.activation(diag_hi[:, k, :], ident[:, :], ACT.Copy, scale=taps_hi[:, k:k + 1].bitcast(F32))
                        act.activation(diag_lo[:, k, :], ident[:, :], ACT.Copy,
                                       scale=taps_lo[:, k:k + 1]).then_inc(diag_ready, 1)
                act.wait_ge(conv_pe_full, 1)
                act.activation(y_a[:, PE_TILE, 0:PROMPT], bank(4 + PE_TILE, 0, PROMPT), ACT.Identity,
                               bias=pcol(PC_BA + PE_TILE)).then_inc(conv_pe_ready, 1)
                prime(ACT.Sqrt)
                for i in range(KA):
                    act.wait_ge(ln_centred, i + 1)
                    act.activation(ln_sq[:, i, :], y_a[:, i, :], ACT.Square).then_inc(ln_squared, 1)
                act.wait_ge(ln_var_full, 1)
                act.activation(rms, bank(5), ACT.Sqrt, bias=eps[:, :], scale=1.0 / DA).then_inc(ln_std_ready, 1)
                prime(ACT.Silu)
                for i in range(KA):
                    act.wait_ge(ln_scaled, i + 1)
                    act.activation(y_a[:, i, :], y_a[:, i, :], ACT.Silu, bias=pcol(PC_LB + i),
                                   scale=pcol(PC_LG + i)).then_inc(y_ready, 1)
                    act.wait_ge(y_ready, KA + i + 1)
                    split_y(i, y_a[:, i, :])
                prime(ACT.Sqrt)
                high(A_BASE + A_UNITS + RING)
                high(A_BASE + A_UNITS + 1 + RING)
                for m in range(KA):
                    norm_tile(2, m)
                high(A_BASE + A_UNITS + 2 + RING)
                for m in range(KA, KD - 1):
                    norm_tile(2, m)
                norm_tile(2, KD - 1)
                high(A_BASE + A_UNITS + 3 + RING)

            def mixer_c():
                for m in range(KD):
                    if m < 6:
                        act.wait_ge(c_full, m // 2 + 1)
                    else:
                        act.wait_ge(w_used, C_BASE + 1)
                    act.activation(sample_of(ext_c, m, HC, 0, HC),
                                   bank(C_BANK[m], T, T + n_hist).rearrange("p (s n) -> p s n", s=SEQS),
                                   ACT.Copy, scale=pcol(PC_PS + m)).then_inc(c_hist_ready, 1)
                    if m == 3:
                        high(C_BASE + RING - 1)
                for m in (0, 1):
                    norm_tile(5, m)
                for tiles in ((2, 3), (4, 5), (6, 7)):
                    for m in tiles:
                        high_part(5, m)
                    for m in tiles:
                        square(5, m)
                    if 4 in tiles:
                        high(C_BASE + RING)

            act.dma_start(par[:, :], a["par"]).then_inc(par_landed, 16)
            act.wait_ge(consts_set, 1)
            prime(ACT.Sqrt)

            def first(c, k):
                act.wait_ge((w_first if k < 2 else w_landed)[c], 32)
                cols = slice(k * 4 * P, (k + 1) * 4 * P)
                act.activation(w_hi[:, c, cols], w_raw[:, c, cols], ACT.Copy).then_inc(first_high if k < 3 else w_high, 1)

            first(0, 0)
            first(0, 1)
            act.wait_ge(par_landed, 16)
            norm_tile(0, 0)
            norm_tile(0, 1)
            first(0, 2)
            first(0, 3)
            norm_tile(0, 2)
            norm_tile(0, 3)
            norm_tile(0, 4)
            first(1, 0)
            first(1, 1)
            norm_tile(0, 5)
            norm_tile(0, 6)
            first(1, 2)
            norm_tile(0, 7)
            first(1, 3)
            first(2, 0)
            root(0)
            for k in range(1, 4):
                first(2, k)
            for k in range(4):
                first(3, k)
            act.activation(taps_hi[:, :], par[:, PE_COLS:PE_COLS + TAPS_A], ACT.Copy).then_inc(taps_high, 1)
            ffn(0)
            mixer_a()
            ffn(1)
            ffn(2)
            mixer_c()
            ffn(3)
            times_g(KD - 2)
            times_g(KD - 1)

        @block.tensor
        def _(pe):
            def product(b, s, col, hi, lo, k, first, last):
                w_h, w_l = w_hi[:, s, col:col + P], w_lo[:, s, col:col + P]
                pe.matmul(bank(b), w_h, hi[:, k, :], start=first, stop=False)
                pe.matmul(bank(b), w_h, lo[:, k, :], start=False, stop=False)
                return pe.matmul(bank(b), w_l, hi[:, k, :], start=False, stop=last)

            def add_square(m):
                pe.wait_ge(squared, KD * 5 + m + 1)
                pe.matmul(bank(stat_bank(5)), ones[:, :], c_square[m], start=m == 0,
                          stop=False).then_inc(square_added, 1)

            def stat(n):
                pe.wait_ge(sum_step, sum_steps(n, KD))
                out = bank(stat_bank(n))
                mm = pe.matmul(out, ones[:, :], c_square[4] if n == 5 else square_sum, start=n != 5,
                               stop=n not in LATE_NORMS)
                if n in LATE_NORMS:
                    pe.wait_ge(squared, KD * (n + 1))
                    mm = pe.matmul(out, ones[:, :], squares[:, (KD - 1) % 2, :], start=False, stop=True)
                mm.then_inc(stat_full, 1)

            def unit_half(c, banks, half, more=0, before_last=None, of=range(4)):
                pe.wait_ge(w_low, c + 1 + more)
                for z in of:
                    g, pair = z % 2, z // 2
                    if z == 3 and before_last is not None:
                        before_last()
                    for k in range(4):
                        mm = product(banks + z, c % RING, (2 * k + g) * 2 * P + pair * P, x_hi, x_lo, 4 * half + k,
                                     half == 0 and k == 0, half == 1 and k == 3)
                    if half == 1 and z == 1:
                        mm.then_inc(pair_full, 1)
                if len(of) == 4:
                    mm.then_inc(w_used, 1)
                return mm

            def by_k_tiles(c, banks, half, before):
                for k in range(4):
                    before(k)
                    for z in range(4):
                        mm = product(banks + z, c % RING, (2 * k + z % 2) * 2 * P + z // 2 * P, x_hi, x_lo, 4 * half + k,
                                     half == 0 and k == 0, half == 1 and k == 3)
                        if half == 1 and k == 3 and z == 1:
                            mm.then_inc(pair_full, 1)
                return mm

            def first(c):
                half, unit = FIRST_IN[0][c]

                def before(k):
                    if c == 1 and k == 1:
                        stat(0)
                    if k < 3:
                        pe.wait_ge(first_low, 3 * c + k + 1)
                    else:
                        pe.wait_ge(w_low, c + 1)
                    if unit == 0:
                        pe.wait_ge(x_low, 4 * half + k + 1)

                by_k_tiles(c, 4 * unit, half, before).then_inc(w_used, 1)

            def ffn(f):
                base, n = FFN_BASE[f], FFN_NORM[f]
                if f == 0:
                    first(0)
                    first(1)
                    pe.wait_ge(rms_ready, 1)
                    first(2)
                    first(3)
                elif f == 3:
                    pe.wait_ge(w_low, base + 1)
                    pe.wait_ge(c_evacuated, 4)

                    def before(k):
                        if k == 2:
                            pe.wait_ge(c_evacuated, 5)
                            add_square(0)
                            add_square(1)
                        pe.wait_ge(x_low, x_low_count(n, k + 1))

                    by_k_tiles(base, 0, 0, before).then_inc(w_used, 1)
                    add_square(2)
                    add_square(3)
                    pe.wait_ge(c_evacuated, KD)
                    unit_half(base + 1, 4, 0, of=range(3))
                    pe.wait_ge(w_low, base + 3)

                    def before(k):
                        if k == 3:
                            stat(n)
                        pe.wait_ge(x_low, x_low_count(n, 4 + k + 1))

                    by_k_tiles(base + 2, 0, 1, before)
                    pe.wait_ge(rms_ready, n + 1)
                    unit_half(base + 1, 4, 0, of=range(3, 4)).then_inc(w_used, 2)
                    unit_half(base + 3, 4, 1)
                else:
                    pe.wait_ge(x_low, x_low_count(n, 4))
                    unit_half(base, 0, 0, before_last=lambda: pe.wait_ge(sum_step, sum_steps(n, KD)))
                    pe.wait_ge(x_low, x_low_count(n, KD))
                    stat(n)
                    unit_half(base + 1, 0, 1)
                if f in (1, 2):
                    pe.wait_ge(r_ready, n + 1)
                    unit_half(base + 2, 4, 0)
                    unit_half(base + 3, 4, 1)
                with pe.Fori(0, UNITS // 2 - 1) as i:
                    for j in range(4, 8):
                        if j % 2 == 0:
                            pe.wait_ge(hid_low, 4 * i + (KF * f + j - 2))
                        unit_half(base + j, 4 * (j // 2 % 2), j % 2, 4 * i)
                pe.wait_ge(hid_low, KF * f + 2 * (UNITS - 2))
                unit_half(base + IN_CHUNKS - 2, 0, 0)
                unit_half(base + IN_CHUNKS - 1, 0, 1)
                base += IN_CHUNKS
                pe.wait_ge(hid_low, KF * f + 2 * (UNITS - 1))
                nn = NEXT_NORM[f]
                with pe.Fori(0, QUARTERS // 2) as i:
                    for q in range(2):
                        if nn in SPLIT_NORMS:
                            pe.wait_ge(x_low, 4 * i + x_low_count(nn, 2 * q - 2))
                        else:
                            pe.wait_ge(x_new, 4 * i + x_new_count(nn, 2 * q - 2))
                        for part, (k0, k1) in enumerate(Q_SPLIT):
                            c = base + 4 * q + part
                            pe.wait_ge(w_low, 8 * i + c + 1)
                            if q == 0 and part == 3:
                                pe.wait_ge(hid_low, KF * (f + 1))
                            for z in range(2):
                                for k in range(k0, k1):
                                    mm = product(4 + 2 * q + z, c % RING, (k - k0) * 2 * P + z * P, h_hi, h_lo, k,
                                                 k == 0, k == KF - 1)
                                if part == 3 and z == 0:
                                    mm.then_inc(out_full, 1)
                            mm.then_inc(w_used, 1)

            def mixer_a():
                for v in range(A_UNITS):
                    c = A_BASE + v
                    banks = 2 * (v % 2)
                    if v == 1:
                        stat(1)
                    if v >= 2:
                        pe.wait_ge(a_evacuated, v - 1)
                    pe.wait_ge(w_low, c + 1)
                    for k in range(KD):
                        if v == 0:
                            pe.wait_ge(x_low, x_low_count(1, k + 1))
                        for z in range(2):
                            mm = product(banks + z, c % RING, (2 * k + z) * P, x_hi, x_lo, k, k == 0, k == KD - 1)
                    mm.then_inc(w_used, 1)
                base = A_BASE + A_UNITS

                def late_part(c):
                    for k in range(KA):
                        pe.wait_ge(y_low, KA + k + 1)
                        for m in range(KA):
                            mm = product(A_OUT_BANK[m], c % RING, k * 512 + m * P, h_hi, h_lo, k, False, k == KA - 1)
                            if k == KA - 1 and m < KA - 1:
                                mm.then_inc(a_out_full, 1)
                    mm.then_inc(w_used, 2)

                def part(c, tiles, k_base, first):
                    for m in tiles:
                        for k in range(KA):
                            mm = product(A_OUT_BANK[m], c % RING, k * 512 + m % 4 * P, h_hi, h_lo, k_base + k,
                                         first and k == 0, not first and k == KA - 1)
                        if not first and m % 4 < 3:
                            mm.then_inc(a_out_full, 1)
                    return mm

                def add_channels(i):
                    if i == PE_TILE:
                        pe.wait_ge(conv_pe_ready, 1)
                    else:
                        pe.wait_ge(conv_prompt, CONV_STEPS * (i + 1))
                    pe.wait_ge(conv_sample, i + 1)
                    return pe.matmul(bank(4), ones[:, :], y_a[:, i, :], start=i == 0, stop=i == KA - 1)

                pe.wait_ge(diag_ready, TAPS_A)
                pe.wait_ge(row_low, 1)
                b = 4 + PE_TILE
                for k in range(TAPS_A):
                    out = bank(b, 0, PROMPT)
                    pe.matmul(out, diag_hi[:, k, :], row_hi[:, k:k + PROMPT], start=k == 0, stop=False)
                    pe.matmul(out, diag_hi[:, k, :], row_lo[:, k:k + PROMPT], start=False, stop=False)
                    mm = pe.matmul(out, diag_lo[:, k, :], row_hi[:, k:k + PROMPT], start=False, stop=k == TAPS_A - 1)
                mm.then_inc(conv_pe_full, 1)
                pe.wait_ge(y_low, KA)
                pe.wait_ge(w_low, base + 1)
                part(base, range(KA), KA, True).then_inc(w_used, 1)
                for i in range(KA):
                    mm = add_channels(i)
                mm.then_inc(ln_sum_full, 1)
                pe.wait_ge(w_low, base + 3)
                part(base + 2, (6,), KA, True)
                for i in range(KA):
                    pe.wait_ge(ln_squared, i + 1)
                    mm = pe.matmul(bank(5), ones[:, :], ln_sq[:, i, :], start=i == 0, stop=i == KA - 1)
                mm.then_inc(ln_var_full, 1)
                pe.wait_ge(conv_pe_ready, 1)
                pe.wait_ge(ln_centred, KA)
                part(base + 2, (7, 4), KA, True)
                pe.wait_ge(ln_std_ready, 1)
                part(base + 2, (5,), KA, True)
                late_part(base + 1)
                pe.wait_ge(w_low, base + 4)
                part(base + 3, range(KA, KD), 0, False).then_inc(w_used, 1)

            def mixer_c():
                pe.wait_ge(w_low, C_BASE + 1)
                pe.wait_ge(hist_c_landed, 16)
                for g in range(4):
                    if g == 3:
                        pe.wait_ge(rms_ready, 5)
                    pe.wait_ge(x_low, x_low_count(4, (2, 4, 8, 8)[g]))
                    for z in range(2):
                        b, s = C_BANK[2 * g + z], C_BASE % RING
                        for k in range(2):
                            i, col = 2 * g + k, (2 * g + k) * 2 * P + z * P
                            product(b, s, col, x_hi, x_lo, i, k == 0, k == 1)
                        if g == 0 and z == 0:
                            stat(4)
                        for k in range(2):
                            i, col = 2 * g + k, (2 * g + k) * 2 * P + z * P
                            mm = pe.matmul(bank(b, T, T + n_hist), w_raw[:, s, col:col + P],
                                           state_c[:, SEQS * i:SEQS * (i + 1), 0:HC], start=k == 0, stop=k == 1)
                    mm.then_inc(c_full if g < 3 else w_used, 1)

            ffn(0)
            mixer_a()
            ffn(1)
            ffn(2)
            mixer_c()
            ffn(3)
            stat(6)

        @block.vector
        def _(dve):
            steps = [0]

            def mark(ins):
                steps[0] += 1
                ins.then_inc(own, 1)

            def settle():
                dve.wait_ge(own, steps[0])

            def close_tile(n, m):
                low_part(n, m)
                add_squares(n, m)

            def low_part(n, m):
                dve.wait_ge(x_high, x_low_count(n, m + 1))
                dve.scalar_tensor_tensor(out=x_lo[:, m, :], in0=x[:, m, :], scalar=pcol(PC_G + KD * n + m),
                                         in1=x_hi[:, m, :].bitcast(F32), op0=ALU.mult,
                                         op1=ALU.subtract).then_inc(x_low, 1)

            def add_squares(n, m):
                last = KD - 2 if n in LATE_NORMS else KD - 1
                if 0 < m <= last:
                    dve.wait_ge(squared, KD * n + m + 1)
                    if m > 1:
                        dve.wait_ge(sum_step, sum_steps(n, m))
                    dst = square_sum if m == last else bank(sum_bank(n))
                    dve.tensor_tensor(dst, bank(sum_bank(n)), squares[:, m % 2, :], ALU.add).then_inc(sum_step, 1)

            def inverse(n, dst):
                dve.wait_ge(rms_ready, n + 1)
                dve.reciprocal(dst, rms).then_inc(r_ready, 1)
                dve.wait_ge(r_ready, n + 1)

            def hidden(f, p, i=0):
                b, z, count = 2 * (p % 4), p % 2, 4 * i + (KF * f + p + 1)
                j = p if isinstance(i, int) else bass.ds(4 * i + p, 1)
                if p % 2 == 0:
                    dve.wait_ge(pair_full, 2 * i + (UNITS * f + p // 2 + 1))
                else:
                    dve.wait_ge(w_used, 4 * i + (FFN_BASE[f] + p + 1))
                dve.tensor_tensor(scaled[:, z, :], bank(b), r[:, :], ALU.mult).then_inc(gate_scaled, 1)
                dve.tensor_tensor(bank(b + 1), bank(b + 1), r[:, :], ALU.mult).then_inc(up_scaled, 1)
                dve.wait_ge(gate_acted, count)
                dve.wait_ge(up_scaled, count)
                dve.tensor_tensor(bank(b), bank(b + 1), acted[:, z, :], ALU.mult).then_inc(hid_ready, 1)
                dve.wait_ge(hid_high, count)
                dve.tensor_tensor(h_lo[:, j, :], bank(b), h_hi[:, j, :].bitcast(F32), ALU.subtract).then_inc(hid_low, 1)

            def ffn(f):
                if f == 3:
                    dve.wait_ge(state_ready, 2)
                inverse(FFN_NORM[f], r[:, :])
                if f == 3:
                    dve.wait_ge(w_used, FFN_BASE[f] + 3)
                with dve.Fori(0, UNITS // 2) as i:
                    for p in range(4):
                        hidden(f, p, i)
                for p in range(4 * (UNITS // 2), KF):
                    hidden(f, p)
                n = NEXT_NORM[f]
                for q in range(QUARTERS):
                    for m in (2 * q, 2 * q + 1):
                        if m % 2 == 0:
                            dve.wait_ge(out_full, QUARTERS * f + q + 1)
                        else:
                            dve.wait_ge(w_used, FFN_BASE[f] + IN_CHUNKS + 4 * (q + 1))
                        dve.scalar_tensor_tensor(out=x[:, m, :], in0=bank(out_bank(m)), scalar=0.5, in1=x[:, m, :],
                                                 op0=ALU.mult, op1=ALU.add).then_inc(x_new, 1)
                        if n in LATE_NORMS:
                            add_squares(n, m)
                    for m in (2 * q, 2 * q + 1):
                        if n == 4:
                            low_part(n, m)
                        elif n != 6:
                            close_tile(n, m)
                    if n == 4 and q == 0:
                        prepare_c()

            def glu(v):
                b = 2 * (v % 2)
                dve.wait_ge(w_used, A_BASE + v + 1)
                dve.tensor_tensor(scaled[:, v % 2, :], bank(b + 1), r[:, :], ALU.mult).then_inc(a_gate_scaled, 1)
                mark(dve.tensor_tensor(bank(b), bank(b), r[:, :], ALU.mult))
                dve.wait_ge(a_gate_acted, v + 1)
                settle()
                mark(dve.tensor_tensor(prompt_of(ext_a, v, HA, HA), bank(b, 0, PROMPT), acted[:, v % 2, 0:PROMPT],
                                       ALU.mult))
                dve.tensor_tensor(sample_of(ext_a, v, HA, HA), sample_cols(bank(b, PROMPT, T)),
                                  sample_cols(acted[:, v % 2, PROMPT:T]), ALU.mult).then_inc(a_evacuated, 1)

            def tap_a(i, k):
                n = CONV_STEPS * i + k
                w = pcol(PC_WA + TAPS_A * i + k)
                src, acc = prompt_of(ext_a, i, HA, k), bank(4 + i, k % 2 * PROMPT, (k % 2 + 1) * PROMPT)
                y = y_a[:, i, 0:PROMPT]
                if k == 0:
                    dve.tensor_scalar(acc, src, w, pcol(PC_BA + i), ALU.mult, ALU.add).then_inc(conv_prompt, 1)
                elif k == 1:
                    dve.tensor_scalar(acc, src, w, None, ALU.mult).then_inc(conv_prompt, 1)
                else:
                    dve.wait_ge(conv_prompt, n - 1)
                    dve.scalar_tensor_tensor(out=y if k == TAPS_A - 1 else acc, in0=src, scalar=w,
                                             in1=acc, op0=ALU.mult, op1=ALU.add).then_inc(conv_prompt, 1)
                if k == TAPS_A - 1:
                    dve.wait_ge(conv_prompt, n + 1)
                    dve.tensor_tensor(y, bank(4 + i, PROMPT, 2 * PROMPT), y, ALU.add).then_inc(conv_prompt, 1)

            def sum_taps(i):
                dve.wait_ge(tap_products, i + 1)
                res = y_a[:, i, PROMPT:T]
                dve.tensor_reduce(sample_cols(res), tap_prod, mybir.AxisListType.X, ALU.add).then_inc(conv_sample_sum, 1)
                dve.wait_ge(conv_sample_sum, i + 1)
                dve.tensor_scalar(res, res, pcol(PC_BA + i), None, ALU.add).then_inc(conv_sample, 1)

            def conv_b(v):
                i, b = v - KA, 2 * (v % 2)
                dve.wait_ge(w_used, A_BASE + v + 1)
                mark(dve.tensor_tensor(scaled[:, v % 2, :], bank(b), r[:, :], ALU.mult))
                mark(dve.tensor_tensor(bank(b + 1), bank(b + 1), r[:, :], ALU.mult))
                settle()
                mark(dve.tensor_tensor(prompt_of(ext_b, i, HB, HB), bank(b + 1, 0, PROMPT), scaled[:, v % 2, 0:PROMPT],
                                       ALU.mult))
                mark(dve.tensor_tensor(sample_of(ext_b, i, HB, HB), sample_cols(bank(b + 1, PROMPT, T)),
                                       sample_cols(scaled[:, v % 2, PROMPT:T]), ALU.mult))
                last = sample_cols(bank(b + 1, PROMPT, T))
                for k in range(TAPS_B):
                    settle()
                    w = pcol(PC_WB + TAPS_B * i + k)
                    for src, acc, res in (
                            (prompt_of(ext_b, i, HB, k), bank(b + 1, 0, PROMPT), y_b[:, i, 0:PROMPT]),
                            (sample_of(ext_b, i, HB, k), last,
                             sample_cols(y_b[:, i, PROMPT:T]))):
                        if k == 0:
                            ins = dve.tensor_scalar(acc, src, w, None, ALU.mult)
                        else:
                            ins = dve.scalar_tensor_tensor(out=res if k == TAPS_B - 1 else acc, in0=src, scalar=w,
                                                           in1=acc, op0=ALU.mult, op1=ALU.add)
                        if acc is not last or k < TAPS_B - 1:
                            mark(ins)
                ins.then_inc(a_evacuated, 1)

            def gate_b(v):
                dve.wait_ge(a_evacuated, 2 * KA)
                dve.wait_ge(w_used, A_BASE + v + 1)
                for t in range(2):
                    b, i = 2 * (v % 2) + t, 2 * (v - 2 * KA) + t
                    mark(dve.tensor_tensor(bank(b), bank(b), r[:, :], ALU.mult))
                    settle()
                    dve.tensor_tensor(bank(b), bank(b), y_b[:, i, :], ALU.mult).then_inc(y_ready, 1)
                for t in range(2):
                    b, i = 2 * (v % 2) + t, 2 * (v - 2 * KA) + t
                    dve.wait_ge(y_high, i + 1)
                    ins = dve.tensor_tensor(h_lo[:, KA + i, :], bank(b), h_hi[:, KA + i, :].bitcast(F32), ALU.subtract)
                    ins.then_inc(y_low, 1)

            def mixer_a():
                inverse(1, r[:, :])
                dve.wait_ge(pads_set, 1)
                dve.wait_ge(hist_ab_landed, 16 * 2 * KA)
                taps = [(i, k) for i in range(PE_TILE) for k in range(TAPS_A)]
                for v in range(A_UNITS):
                    (glu if v < KA else conv_b if v < 2 * KA else gate_b)(v)
                    if v in SUM_AT:
                        sum_taps(SUM_AT.index(v))
                    for _ in range(TAPS_BETWEEN[0 if v < KA else 1 if v < 2 * KA else 2]):
                        if taps and taps[0][0] <= v:
                            i, k = taps.pop(0)
                            if k == 0:
                                dve.wait_ge(a_evacuated, i + 1)
                                settle()
                            tap_a(i, k)
                for i, k in taps:
                    if k == 0:
                        dve.wait_ge(a_evacuated, i + 1)
                    tap_a(i, k)
                sum_taps(KA - 1)
                dve.wait_ge(ln_sum_full, 1)
                for i in range(KA):
                    dve.scalar_tensor_tensor(out=y_a[:, i, :], in0=bank(4), scalar=-1.0 / DA, in1=y_a[:, i, :],
                                             op0=ALU.mult, op1=ALU.add).then_inc(ln_centred, 1)
                dve.wait_ge(ln_std_ready, 1)
                mark(dve.reciprocal(inverse_std, rms))
                settle()
                for i in range(KA):
                    dve.tensor_tensor(y_a[:, i, :], y_a[:, i, :], inverse_std, ALU.mult).then_inc(ln_scaled, 1)
                for i in range(KA):
                    dve.wait_ge(y_high, KA + i + 1)
                    dve.tensor_tensor(h_lo[:, i, :], y_a[:, i, :], h_hi[:, i, :].bitcast(F32),
                                      ALU.subtract).then_inc(y_low, 1)
                def add_out(m):
                    if m % 4 == 3:
                        dve.wait_ge(w_used, A_BASE + A_UNITS + m // 4 * 2 + 2)
                    else:
                        dve.wait_ge(a_out_full, 3 * (m // 4) + m % 4 + 1)
                    dve.tensor_tensor(x[:, m, :], bank(A_OUT_BANK[m]), x[:, m, :], ALU.add).then_inc(x_new, 1)
                for m in range(KD):
                    add_out(m)
                    if m > 0:
                        close_tile(2, m - 1)
                close_tile(2, KD - 1)

            def prepare_c():
                dve.wait_ge(a_state_out, 16 * 4 * KA)
                mark(dve.memset(ext_c[:, :, 0:HC], 0.0))
                dve.wait_ge(count_set, 1)
                mark(dve.tensor_copy(inv_count[:, 0, :], count_i[:, :]))
                settle()
                for g in (3, 2, 1, 0):
                    mark(dve.tensor_scalar(inv_count[:, g, :], inv_count[:, 0, :], float(WINDOWS[g]), None, ALU.min))
                settle()
                mark(dve.reciprocal(inv_count[:, :, :], inv_count[:, :, :]))
                mark(dve.tensor_tensor(bias_scaled[:, :], par[:, PC_PB:PC_PB + KD], par[:, PC_PS:PC_PS + KD], ALU.mult))

            def mixer_c():
                inverse(4, r[:, :])
                settle()

                def scaled_out(m):
                    b, ps = C_BANK[m], pcol(PC_PS + m)
                    dve.wait_ge(c_hist_ready, m + 1)
                    mark(dve.scalar_tensor_tensor(out=prompt_of(ext_c, m, HC, HC), in0=bank(b, 0, PROMPT), scalar=ps,
                                                  in1=r[:, 0:PROMPT], op0=ALU.mult, op1=ALU.mult))
                    dve.scalar_tensor_tensor(out=sample_of(ext_c, m, HC, HC), in0=sample_cols(bank(b, PROMPT, T)),
                                             scalar=ps, in1=sample_cols(r[:, PROMPT:T]), op0=ALU.mult,
                                             op1=ALU.mult).then_inc(c_evacuated, 1)

                def less_own(m):
                    bias = bias_scaled[:, m:m + 1]
                    mark(dve.scalar_tensor_tensor(out=x[:, m, 0:PROMPT], in0=x[:, m, 0:PROMPT], scalar=bias,
                                                  in1=prompt_of(ext_c, m, HC, HC), op0=ALU.add, op1=ALU.subtract))
                    mark(dve.scalar_tensor_tensor(out=sample_cols(x[:, m, PROMPT:T]), in0=sample_cols(x[:, m, PROMPT:T]),
                                                  scalar=bias, in1=sample_of(ext_c, m, HC, HC), op0=ALU.add,
                                                  op1=ALU.subtract))

                def windows(g):
                    settle()
                    src, n, z = ext_pair[g], 1, 0
                    while n < WINDOWS[g]:
                        first = 2 * n - 1
                        mark(dve.tensor_tensor(win[z][:, :, first:ec_w], src[:, :, first:ec_w],
                                               src[:, :, first - n:ec_w - n], ALU.add))
                        if n == 1:
                            less_own(2 * g)
                            less_own(2 * g + 1)
                        settle()
                        src, n, z = win[z], 2 * n, 1 - z
                    return src

                def add_means(g, sums):
                    settle()
                    both = slice(2 * g, 2 * g + 2)
                    counts = inv_count[:, g, :].unsqueeze(1).broadcast_to([P, 2, HC])
                    mark(dve.tensor_tensor(head[:, :, :], sums[:, :, HC:2 * HC], counts, ALU.mult))
                    mark(dve.scalar_tensor_tensor(out=x[:, both, HC:PROMPT], in0=sums[:, :, 2 * HC:HC + PROMPT],
                                                  scalar=1.0 / WINDOWS[g], in1=x[:, both, HC:PROMPT],
                                                  op0=ALU.mult, op1=ALU.add))
                    for t, m in enumerate((2 * g, 2 * g + 1)):
                        mark(dve.scalar_tensor_tensor(out=sample_cols(x[:, m, PROMPT:T]), in0=sample_of(sums, t, HC, HC),
                                                      scalar=1.0 / WINDOWS[g], in1=sample_cols(x[:, m, PROMPT:T]),
                                                      op0=ALU.mult, op1=ALU.add))
                    dve.wait_ge(own, steps[0] - 3)
                    dve.tensor_tensor(x[:, both, 0:HC], head[:, :, :], x[:, both, 0:HC], ALU.add).then_inc(x_new, 2)

                for m in range(4):
                    scaled_out(m)
                dve.wait_ge(c_evacuated, 2)
                add_means(0, windows(0))
                less_own(2)
                less_own(3)
                low_part(5, 0)
                low_part(5, 1)
                scaled_out(6)
                scaled_out(7)
                dve.wait_ge(window_step, 2)
                add_means(1, win_raw)
                scaled_out(4)
                low_part(5, 2)
                low_part(5, 3)
                scaled_out(5)
                dve.wait_ge(c_evacuated, KD)
                add_means(2, windows(2))
                less_own(6)
                less_own(7)
                low_part(5, 4)
                low_part(5, 5)
                dve.wait_ge(window_step, 6)
                add_means(3, pool_win[3][-1])
                low_part(5, 6)
                low_part(5, 7)
                dve.wait_ge(squared, KD * 6)
                mark(dve.tensor_tensor(norm_buf[:, 0:2, :], norm_buf[:, 0:2, :], norm_buf[:, 2:4, :], ALU.add))
                settle()
                dve.tensor_tensor(c_square[4], c_square[4], c_square[5], ALU.add).then_inc(sum_step, KD - 1)

            def final():
                dve.wait_ge(rms_ready, 7)
                dve.reciprocal(r[:, 0:T // 2], rms[:, 0:T // 2]).then_inc(half_r, 1)
                dve.wait_ge(half_r, 1)
                dve.wait_ge(y_times_g, KD)
                times_r(dve, 0, 0).then_inc(y_done, 1)
                dve.reciprocal(r[:, T // 2:T], rms[:, T // 2:T]).then_inc(r_ready, 1)
                dve.wait_ge(r_ready, 7)
                for part in (0, 1):
                    times_r(dve, part, 1).then_inc(y_done, 1)

            dve.wait_ge(par_landed, 16)
            for m in range(KD):
                close_tile(0, m)
            ffn(0)
            mixer_a()
            ffn(1)
            ffn(2)
            mixer_c()
            ffn(3)
            final()


TAPS_BETWEEN = (10, 5, 9)
PE_TILE = KA - 1
PE_COLS = PC_WA + TAPS_A * PE_TILE
DIAGS_AT_ONCE = 5
CONV_STEPS = TAPS_A + 1
SUM_AT = (4, 6, 8)
ROW_AT = 9
PRODUCTS_AT = (6, 8, 10, 12)

INPUTS = {
    "x_t": (P, KD, T), "par": (P, PARAMS), "hist_a": (P, KA, SEQS, HA), "hist_b": (P, KA, SEQS, HB),
    "hist_c": (P, KD, SEQS, HC), "ffn_w_in": (2, 2, D, 2 * DFF), "ffn_w_out": (2, 2, DFF, D),
    "mix_w_in": (1, D, 5 * DA), "mix_w_out": (1, D, D), "pool_w": (1, 4, 256, 256),
}
OUTPUTS = {
    "y_t": (P, KD, T), "new_a_prompt": (P, KA, HA), "new_a_sample": (P, KA, SEQS, HA),
    "new_b_prompt": (P, KA, HB), "new_b_sample": (P, KA, SEQS, HB),
    "new_c_prompt": (P, KD, HC), "new_c_sample": (P, KD, SEQS, HC),
}


def kernel(**inputs):
    import numpy as np
    from concourse import bacc
    from concourse.bass_utils import run_bass_kernel_spmd

    g = {k: np.asarray(v) for k, v in inputs.items()}

    def by_partition(v):
        v = v.reshape(*v.shape[:-1], v.shape[-1] // P, P)
        return np.moveaxis(v, -1, 0)

    tokens = np.concatenate([g["x_prompt"].reshape(PROMPT, D), g["x_sample"].reshape(SEQS * STEP, D)])
    par = np.concatenate([
        by_partition(g["norm_g"]).reshape(P, 6 * KD),
        by_partition(g["final_norm_g"]),
        by_partition(g["conv_a_w"][0]).transpose(0, 2, 1).reshape(P, KA * TAPS_A),
        by_partition(g["conv_a_b"][0]), by_partition(g["ln_a_g"][0]), by_partition(g["ln_a_b"][0]),
        by_partition(g["conv_b_w"][0]).transpose(0, 2, 1).reshape(P, KA * TAPS_B),
        by_partition(g["pool_b"][0]), by_partition(g["pool_scale"][0]),
    ], axis=1)

    def history(v):
        return by_partition(v).transpose(0, 3, 1, 2)

    data = {
        "x_t": by_partition(tokens).transpose(0, 2, 1), "par": par,
        "hist_a": history(g["state_conv_a"][0]), "hist_b": history(g["state_conv_b"][0]),
        "hist_c": history(g["state_pool"][0]),
        "ffn_w_in": g["ffn_w_in"], "ffn_w_out": g["ffn_w_out"], "mix_w_in": g["mix_w_in"],
        "mix_w_out": g["mix_w_out"], "pool_w": g["pool_w"],
    }
    data = {k: np.ascontiguousarray(v) for k, v in data.items()}

    nc = bacc.Bacc("TRN2", target_bir_lowering=False, num_devices=1)
    aps = {k: nc.dram_tensor(k, s, F32, kind="ExternalInput").ap() for k, s in INPUTS.items()}
    aps |= {k: nc.dram_tensor(k, s, F32, kind="ExternalOutput").ap() for k, s in OUTPUTS.items()}
    build(nc, aps)
    got = run_bass_kernel_spmd(nc, [data], core_ids=[0]).results[0]

    y = got["y_t"].transpose(2, 1, 0).reshape(T, D)

    def prompt_rows(v):
        return np.ascontiguousarray(v.transpose(2, 1, 0).reshape(1, 1, v.shape[2], -1))

    def sample_rows(v):
        return np.ascontiguousarray(v.transpose(2, 3, 1, 0).reshape(1, SEQS, v.shape[3], -1))

    return (np.ascontiguousarray(y[:PROMPT].reshape(1, PROMPT, D)),
            np.ascontiguousarray(y[PROMPT:].reshape(SEQS, STEP, D)),
            prompt_rows(got["new_a_prompt"]), prompt_rows(got["new_b_prompt"]), prompt_rows(got["new_c_prompt"]),
            sample_rows(got["new_a_sample"]), sample_rows(got["new_b_sample"]), sample_rows(got["new_c_sample"]))
```
